# Optimizing a Trainium2 kernel written in Bass

```python
import jax, jax.numpy as jnp
from jax import lax
import numpy as np

D_MODEL = 1024
BATCH = 1
SEQ = 2048
DEPTH = 2
DEC_BATCH = 8
DEC_SEQ = 1
PAST_LEN = 16384
PAGE_SIZE = 128

MIX_WIDTH = D_MODEL
GLA_WIDTH = MIX_WIDTH // 2
RET_WIDTH = MIX_WIDTH - GLA_WIDTH
GLA_HEADS = 4
GLA_DV = GLA_WIDTH // GLA_HEADS
GLA_DK = GLA_DV // 2
GLA_RANK = 16
GLA_GATE_TAU = 16.0
RET_HEADS = 4
RET_DV = RET_WIDTH // RET_HEADS
RET_DK = RET_DV // 2
IN_COLS = (2 * GLA_HEADS * GLA_DK + 2 * GLA_WIDTH + GLA_RANK
           + 2 * RET_HEADS * RET_DK + 2 * RET_WIDTH)
CHUNK = 64
ROPE_BASE = 10000.0
EPS = 1e-6
GN_EPS = 1e-5

kernel_name = 'hymba_gla_retnet_hybrid_step'

F32 = jnp.float32

def _rmsnorm(x, w):
    xf = x.astype(F32)
    y = xf * lax.rsqrt(jnp.mean(xf * xf, axis=-1, keepdims=True) + EPS) * w.astype(F32)
    return y.astype(x.dtype)

def _split_cols(z):
    sizes = (GLA_HEADS * GLA_DK, GLA_HEADS * GLA_DK, GLA_WIDTH, GLA_WIDTH, GLA_RANK,
             RET_HEADS * RET_DK, RET_HEADS * RET_DK, RET_WIDTH, RET_WIDTH)
    offs = np.cumsum(sizes)[:-1].tolist()
    return jnp.split(z, offs, axis=-1)

def _rope(x, pos):
    half = x.shape[-1] // 2
    inv = ROPE_BASE ** (-jnp.arange(half, dtype=F32) / half)
    ang = pos.astype(F32)[:, None] * inv[None, :]
    cos = jnp.cos(ang)[:, None, :]
    sin = jnp.sin(ang)[:, None, :]
    x1, x2 = x[..., :half], x[..., half:]
    return jnp.concatenate([x1 * cos - x2 * sin, x1 * sin + x2 * cos], axis=-1)

def _ret_log_gamma():
    return jnp.log(1.0 - jnp.power(2.0, -5.0 - jnp.arange(RET_HEADS, dtype=F32)))

def _to_chunks(a):
    b, t, h, d = a.shape
    return a.reshape(b, t // CHUNK, CHUNK, h, d).transpose(1, 0, 3, 2, 4)

def _from_chunks(o):
    n, b, h, c, d = o.shape
    return o.transpose(1, 0, 3, 2, 4).reshape(b, n * c, h, d)

def _gla_chunked(q, k, v, la, s0):
    mask = jnp.tril(jnp.ones((CHUNK, CHUNK), dtype=bool))

    def step(s, xs):
        qc, kc, vc, lc = xs
        b = jnp.cumsum(lc, axis=2)
        qd = qc * jnp.exp(b)
        kd = kc * jnp.exp(-b)
        att = jnp.where(mask, jnp.einsum('bhtk,bhsk->bhts', qd, kd), 0.0)
        o = jnp.einsum('bhts,bhsv->bhtv', att, vc) + jnp.einsum('bhtk,bhkv->bhtv', qd, s)
        b_last = b[:, :, -1:, :]
        s_new = (jnp.exp(b_last[:, :, 0, :])[..., None] * s
                 + jnp.einsum('bhsk,bhsv->bhkv', kc * jnp.exp(b_last - b), vc))
        return s_new, o

    s, o = lax.scan(step, s0, (_to_chunks(q), _to_chunks(k), _to_chunks(v), _to_chunks(la)))
    return _from_chunks(o), s

def _gla_recurrent(q, k, v, la, s0):
    def step(s, xs):
        qt, kt, vt, lt = xs
        s = jnp.exp(lt)[..., None] * s + kt[..., None] * vt[..., None, :]
        return s, jnp.einsum('bhk,bhkv->bhv', qt, s)

    s, o = lax.scan(step, s0, (q.swapaxes(0, 1), k.swapaxes(0, 1), v.swapaxes(0, 1), la.swapaxes(0, 1)))
    return o.swapaxes(0, 1), s

def _ret_chunked(q, k, v, s0):
    lg = _ret_log_gamma()
    idx = jnp.arange(CHUNK, dtype=F32)
    rel = idx[:, None] - idx[None, :]
    dmat = jnp.where(rel >= 0, jnp.exp(lg[:, None, None] * jnp.maximum(rel, 0.0)), 0.0)
    q_dec = jnp.exp(lg[:, None] * (idx + 1.0)[None, :])[None, :, :, None]
    k_dec = jnp.exp(lg[:, None] * (CHUNK - 1.0 - idx)[None, :])[None, :, :, None]
    chunk_dec = jnp.exp(lg * CHUNK)[None, :, None, None]

    def step(s, xs):
        qc, kc, vc = xs
        att = jnp.einsum('bhtk,bhsk->bhts', qc, kc) * dmat[None]
        o = jnp.einsum('bhts,bhsv->bhtv', att, vc) + jnp.einsum('bhtk,bhkv->bhtv', qc * q_dec, s)
        s_new = chunk_dec * s + jnp.einsum('bhsk,bhsv->bhkv', kc * k_dec, vc)
        return s_new, o

    s, o = lax.scan(step, s0, (_to_chunks(q), _to_chunks(k), _to_chunks(v)))
    return _from_chunks(o), s

def _ret_recurrent(q, k, v, s0):
    gamma = jnp.exp(_ret_log_gamma())[None, :, None, None]

    def step(s, xs):
        qt, kt, vt = xs
        s = gamma * s + kt[..., None] * vt[..., None, :]
        return s, jnp.einsum('bhk,bhkv->bhv', qt, s)

    s, o = lax.scan(step, s0, (q.swapaxes(0, 1), k.swapaxes(0, 1), v.swapaxes(0, 1)))
    return o.swapaxes(0, 1), s

def _layer(x, pos, s_gla, s_ret, norm_w, w_in, gla_w2, gla_b, gla_norm_w,
           ret_norm_w, ret_norm_b, w_out, chunked):
    B, T, _ = x.shape
    h = _rmsnorm(x, norm_w)
    z = jnp.einsum('btd,dc->btc', h, w_in).astype(F32)
    gq, gk, gv, gg, glr, rq, rk, rv, rg = _split_cols(z)
    q_a = gq.reshape(B, T, GLA_HEADS, GLA_DK) * (GLA_DK ** -0.5)
    k_a = gk.reshape(B, T, GLA_HEADS, GLA_DK)
    v_a = gv.reshape(B, T, GLA_HEADS, GLA_DV)
    la = (jax.nn.log_sigmoid(glr @ gla_w2.astype(F32) + gla_b.astype(F32)) / GLA_GATE_TAU
          ).reshape(B, T, GLA_HEADS, GLA_DK)
    q_b = _rope(rq.reshape(B, T, RET_HEADS, RET_DK), pos)
    k_b = _rope(rk.reshape(B, T, RET_HEADS, RET_DK), pos) * (RET_DK ** -0.5)
    v_b = rv.reshape(B, T, RET_HEADS, RET_DV)
    if chunked:
        o_a, s_gla_new = _gla_chunked(q_a, k_a, v_a, la, s_gla)
        o_b, s_ret_new = _ret_chunked(q_b, k_b, v_b, s_ret)
    else:
        o_a, s_gla_new = _gla_recurrent(q_a, k_a, v_a, la, s_gla)
        o_b, s_ret_new = _ret_recurrent(q_b, k_b, v_b, s_ret)
    o_a = o_a * lax.rsqrt(jnp.mean(o_a * o_a, axis=-1, keepdims=True) + EPS) * gla_norm_w.astype(F32)
    o_a = o_a.reshape(B, T, GLA_WIDTH) * jax.nn.silu(gg)
    mu = jnp.mean(o_b, axis=-1, keepdims=True)
    var = jnp.mean(jnp.square(o_b - mu), axis=-1, keepdims=True)
    o_b = ((o_b - mu) * lax.rsqrt(var + GN_EPS)).reshape(B, T, RET_WIDTH)
    o_b = (o_b * ret_norm_w.astype(F32) + ret_norm_b.astype(F32)) * jax.nn.silu(rg)
    mixed = jnp.concatenate([o_a, o_b], axis=-1).astype(x.dtype)
    y = x + jnp.einsum('btc,cd->btd', mixed, w_out)
    return y, s_gla_new, s_ret_new

def setup_inputs(seed: int = 0) -> dict:
    key = jax.random.key(seed)
    ks = jax.random.split(key, 14)
    nrm = jax.random.normal
    return {
        'x_prompt': nrm(ks[0], (BATCH, SEQ, D_MODEL), F32),
        'x_sample': nrm(ks[1], (DEC_BATCH, DEC_SEQ, D_MODEL), F32),
        'state_gla': nrm(ks[2], (DEPTH, DEC_BATCH, GLA_HEADS, GLA_DK, GLA_DV), F32),
        'state_ret': nrm(ks[3], (DEPTH, DEC_BATCH, RET_HEADS, RET_DK, RET_DV), F32),
        'norm_w': 1.0 + 0.05 * nrm(ks[4], (DEPTH, D_MODEL), F32),
        'w_in': nrm(ks[5], (DEPTH, D_MODEL, IN_COLS), F32) * D_MODEL ** -0.5,
        'gla_w2': nrm(ks[6], (DEPTH, GLA_RANK, GLA_HEADS * GLA_DK), F32) * GLA_RANK ** -0.5,
        'gla_b': 0.1 * nrm(ks[7], (DEPTH, GLA_HEADS * GLA_DK), F32),
        'gla_norm_w': 1.0 + 0.05 * nrm(ks[8], (DEPTH, GLA_DV), F32),
        'ret_norm_w': 1.0 + 0.05 * nrm(ks[9], (DEPTH, RET_WIDTH), F32),
        'ret_norm_b': 0.02 * nrm(ks[10], (DEPTH, RET_WIDTH), F32),
        'w_out': nrm(ks[11], (DEPTH, MIX_WIDTH, D_MODEL), F32) * MIX_WIDTH ** -0.5,
        'final_norm_w': 1.0 + 0.05 * nrm(ks[12], (D_MODEL,), F32),
    }

def reference(x_prompt, x_sample, state_gla, state_ret, norm_w, w_in, gla_w2, gla_b,
              gla_norm_w, ret_norm_w, ret_norm_b, w_out, final_norm_w):
    bp, tp, _ = x_prompt.shape
    bs, ts, _ = x_sample.shape
    pos_p = jnp.arange(tp, dtype=jnp.int32)
    pos_s = PAST_LEN + jnp.arange(ts, dtype=jnp.int32)
    hp, hs = x_prompt, x_sample
    gla_p, ret_p, gla_s, ret_s = [], [], [], []
    for l in range(DEPTH):
        w = (norm_w[l], w_in[l], gla_w2[l], gla_b[l], gla_norm_w[l], ret_norm_w[l], ret_norm_b[l], w_out[l])
        z_gla = jnp.zeros((bp, GLA_HEADS, GLA_DK, GLA_DV), F32)
        z_ret = jnp.zeros((bp, RET_HEADS, RET_DK, RET_DV), F32)
        hp, sg, sr = _layer(hp, pos_p, z_gla, z_ret, *w, chunked=True)
        gla_p.append(sg)
        ret_p.append(sr)
        hs, sg, sr = _layer(hs, pos_s, state_gla[l].astype(F32), state_ret[l].astype(F32), *w, chunked=False)
        gla_s.append(sg)
        ret_s.append(sr)
    y_prompt = _rmsnorm(hp, final_norm_w)
    y_sample = _rmsnorm(hs, final_norm_w)
    gla_state_prompt = jnp.stack(gla_p).astype(state_gla.dtype)
    ret_state_prompt = jnp.stack(ret_p).astype(state_ret.dtype)
    gla_state_sample = jnp.stack(gla_s).astype(state_gla.dtype)
    ret_state_sample = jnp.stack(ret_s).astype(state_ret.dtype)
    return (y_prompt, y_sample, gla_state_prompt, ret_state_prompt, gla_state_sample, ret_state_sample)


_drawn_inputs = setup_inputs


def setup_inputs(seed=0):
    import zlib

    import numpy as np

    out = dict(_drawn_inputs(seed))
    spreads = {}
    factors = {'ret_norm_b': 5.104}
    for name, (base, spread) in spreads.items():
        noise = np.random.default_rng([zlib.crc32(name.encode()), seed]).standard_normal(out[name].shape)
        drawn = base * np.exp(spread * noise) if base else spread * noise
        out[name] = __import__('jax').numpy.asarray(drawn.astype(out[name].dtype))
    for name, factor in factors.items():
        out[name] = (out[name] * factor).astype(out[name].dtype)
    return out
```

```python
from contextlib import ExitStack

import numpy as np

import concourse.bass as bass
from concourse import mybir

D, SEQ, DEPTH, DECB, PAST = 1024, 2048, 2, 8, 16384
HEADS, DK, DV, RANK = 4, 64, 128, 16
EPS, GN_EPS, TAU, ROPE_BASE = 1e-6, 1e-5, 16.0, 10000.0
TOK = 128
BLK = 512
TPB = BLK // TOK
NBLK = SEQ // BLK
KT = D // 128
SLOTS = 33
RING = 3
AHEAD = 2
MIX_ORDER = (15, 16, 17, 18, 26, 26, 27, 27)
Z_BANK = "SSXSSX"
Z_READ = (5, 9, 13, 17, 21, 25)
V_AT = tuple(range(8)) + tuple(range(11, 19))
V_H, V_LA, V_QR, V_QG = 3, 4, 9, 10
V_DEC = (11, 21)
V_O = (20, 30)
V_SQ, V_MOM, V_VAR, V_MIX, V_X0, V_X1, V_NV, V_LAST = 31, 34, 35, 42, 43, 44, 48, 50
MID = TOK // 2 - 1


class Count:

    def __init__(self, sem, per, base=0):
        self.sem, self.per, self.base = sem, per, base

    def at(self, n, k):
        return n * self.per + (self.base + k)


def build(nc, d):
    f32, f32r, u8 = mybir.dt.float32, mybir.dt.float32r, mybir.dt.uint8
    ALU, ACT = mybir.AluOpType, mybir.ActivationFunctionType
    ctx = ExitStack()
    with ctx:
        def sb(name, shape, dt=f32):
            return ctx.enter_context(nc.sbuf_tensor(name, shape, dt))

        def sem(name):
            return ctx.enter_context(nc.semaphore(name))

        w_stage = sb("w_stage", [128, RING, 512])
        w_lo = sb("w_lo", [128, RING, 1024], f32r)
        w_hi = sb("w_hi", [128, RING, 1024], f32r)
        xn = sb("xn", [128, TPB, D])
        h_hi = sb("h_hi", [128, KT, BLK], f32r)
        h_lo = sb("h_lo", [128, KT, BLK], f32r)
        m_hi = sb("m_hi", [128, KT, BLK], f32r)
        m_lo = sb("m_lo", [128, KT, BLK], f32r)
        region = sb("region", [128, 9216])
        q_t = region[:, 0:2048].rearrange("p (i h n) -> p i h n", i=2, h=2)
        v_n = region[:, 2048:4096].rearrange("p (t n) -> p t n", t=TPB)
        y_t = region[:, 0:4096].rearrange("p (t n) -> p t n", t=TPB)
        g_t = region[:, 4096:6144].rearrange("p (h n) -> p h n", h=HEADS)
        o_n = region[:, 6144:8192].rearrange("p (t n) -> p t n", t=TPB)
        yn = region[:, 4096:8192].rearrange("p (t n) -> p t n", t=TPB)
        k_t = region[:, 8192:9216].rearrange("p (i n) -> p i n", i=2)
        rope = sb("rope", [128, 2, BLK])
        ex = sb("ex", [128, 2, 2, BLK])
        fin_w = ex[:, 0, :, :].rearrange("p a n -> p (a n)")
        em = sb("em", [128, TPB, 2, 2])
        cc = sb("cc", [128, 2, TPB])
        spare = sb("spare", [128, 64])
        la = sb("la", [128, TPB, 256])
        tmp = sb("tmp", [128, 2, BLK])
        r_tmp = tmp[:, 0, :]
        lr_t = k_t[0:32, 0, :]
        k_n = sb("k_n", [128, TPB, 256])
        a_ret = tmp[:, 1, :].rearrange("p (h n) -> p h n", h=HEADS)
        a_gla = sb("a_gla", [128, HEADS, TOK])
        s_ret = sb("s_ret", [128, 512])
        s_gla = sb("s_gla", [128, 512])
        s_mid = sb("s_mid", [128, 512])
        bns = sb("bns", [128, 2, HEADS, 6])
        agg = sb("agg", [128, 2, HEADS, 2])
        msq = sb("msq", [128, 2, HEADS])
        var = sb("var", [128, 2, HEADS])
        rstd = sb("rstd", [128, 2, HEADS])
        xbn = sb("xbn", [128, TPB, 12])
        xagg = sb("xagg", [128, TPB, 2])
        xms = sb("xms", [128, TPB])
        xvar = sb("xvar", [128, TPB])
        xrs = sb("xrs", [128, TPB])
        yrs = sb("yrs", [128, TPB])
        ident = sb("ident", [128, 128])
        cum = sb("cum", [128, 130])
        gmask = sb("gmask", [128, TOK], u8)
        rmask = sb("rmask", [128, HEADS * TOK])
        kdec = sb("kdec", [128, HEADS])
        qdec = sb("qdec", [128, 2, TOK])
        small = sb("small", [128, 16])
        half = sb("half", [128, 64])
        nw = sb("nw", [128, KT])
        par = sb("par", [128, 17])
        parh = sb("parh", [128, 9])
        w2b = sb("w2b", [RANK + 1, 256])
        comb = sb("comb", [16, 8])
        ones = sb("ones", [128, 128])
        ss = sb("ss", [128, 2, DECB, DV])
        ys = ss[0:8, 0, :, :].rearrange("p b n -> p (b n)")
        z_u = sb("z_u", [16, 512])
        z_v = sb("z_v", [16, 2, 512])
        xs = sb("xs", [8, D])
        xsn = z_v[0:8, :, :].rearrange("p a n -> p (a n)")
        hs = sb("hs", [128, KT, 16], f32r)
        ms = sb("ms", [128, KT, 16], f32r)
        lr_s = sb("lr_s", [32, 8])
        z_t = sb("z_t", [128, 16, 8])
        rot = sb("rot", [128, 4, 8])
        gt, al, hs_f = sb("gt", [128, 16]), sb("al", [128, 16]), sb("hs_f", [128, 64])
        q_s = sb("q_s", [128, 2, 2, 8, 2])
        k_s = sb("k_s", [128, 2, 2, 8])
        o_s = sb("o_s", [128, 2, 64])
        v_s = sb("v_s", [128, 2, 64])
        sg_s, rs_s = sb("sg_s", [128, 64]), sb("rs_s", [128, 64])
        sbn, sagg = sb("sbn", [8, 12]), sb("sagg", [8, 2])
        smsq, svar, srs = sb("smsq", [8, 1]), sb("svar", [8, 1]), sb("srs", [8, 1])

        bank = [ctx.enter_context(nc.psum_tensor(f"bank{i}", [128, 512], f32)) for i in range(8)]
        P, ATT, OB, ST, X = bank[0:4], bank[4], bank[5], bank[6], bank[7]

        w_loaded = [sem(f"w_loaded{r}") for r in range(RING)]
        hi_done, lo_done, slot_used = sem("hi_done"), sem("lo_done"), sem("slot_used")
        const_in, par_in, sets = sem("const_in"), sem("par_in"), sem("sets")
        x_in, nw_in, rope_in, res_in, fin_in = (Count(sem(n), 16) for n in ("x_in", "nw_in", "rope_in", "res_in", "fin_in"))
        stored = Count(sem("stored"), 16, base=16)
        state_in, state_out, st_saved = sem("state_in"), sem("state_out"), sem("st_saved")
        proj = Count(sem("proj"), 24)
        gate_x, cum_b, mid_b = Count(sem("gate_x"), 2), Count(sem("cum_b"), 2), Count(sem("mid_b"), 1)
        kn_ps, kn_sb = Count(sem("kn_ps"), 4), Count(sem("kn_sb"), 4)
        att_ps, o_ps, st_ps, mt_ps = (Count(sem(n), 8) for n in ("att_ps", "o_ps", "st_ps", "mt_ps"))
        ht_ps = Count(sem("ht_ps"), 8)
        lr_sb, gate_l, ex_sb, em_sb = Count(sem("lr_sb"), 1), Count(sem("gate_l"), 6), Count(sem("ex_sb"), 4), Count(sem("em_sb"), 1)
        k_raw, v_sb, g_tanh, o_sb = Count(sem("k_raw"), 2), Count(sem("v_sb"), 8), Count(sem("g_tanh"), 8), Count(sem("o_sb"), 8)
        m_aff, mhi_sb, hhi_sb = Count(sem("m_aff"), 4), Count(sem("mhi_sb"), 8), Count(sem("hhi_sb"), 8)
        lr_ones = Count(sem("lr_ones"), 1)
        la_sb, q_raw, rope_st, qk_gla = Count(sem("la_sb"), 2), Count(sem("q_raw"), 2), Count(sem("rope_st"), 18), Count(sem("qk_gla"), 4)
        att_sb, sret_sb = Count(sem("att_sb"), 8), Count(sem("sret_sb"), 4)
        sgla_sb, cc_sb = Count(sem("sgla_sb"), 9), Count(sem("cc_sb"), 1)
        ostat, normed, g_silu = Count(sem("ostat"), 28), Count(sem("normed"), 8), Count(sem("g_silu"), 8)
        mix_sb, y_add, hlo_sb = Count(sem("mix_sb"), 8), Count(sem("y_add"), 8, base=8), Count(sem("hlo_sb"), 8)
        xstat, xn_sb, ystat, yn_sb = Count(sem("xstat"), 4), Count(sem("xn_sb"), 1), Count(sem("ystat"), 4), Count(sem("yn_sb"), 1)
        rstd_o, rstd_x, rstd_y, mlo_sb = Count(sem("rstd_o"), 8), Count(sem("rstd_x"), 1), Count(sem("rstd_y"), 1), Count(sem("mlo_sb"), 8)
        s_v = Count(sem("s_v"), V_LAST, base=6)
        s_p = Count(sem("s_p"), 2, base=1)
        xs_t, zt_ps, gx_ps, vb_ps = (Count(sem(n), k) for n, k in (("xs_t", 1), ("zt_ps", 5), ("gx_ps", 1), ("vb_ps", 16)))
        so_ps, mom_ps = Count(sem("so_ps"), 2), Count(sem("mom_ps"), 1)
        z_sb, zt_sb, gl_s, al_s, tg_s = (Count(sem(n), k) for n, k in (("z_sb", 7), ("zt_sb", 5), ("gl_s", 3), ("al_s", 1), ("tg_s", 2)))
        fin_out = sem("fin_out")

        columns = iter(range(64))

        def apart():
            c = next(columns)
            nc.vector.memset(spare[:, c:c + 1], 0.0)

        def load_half(act, first_row, n, h):
            act.wait_ge(lo_done, n * 2 * SLOTS + (h + 1))
            act.dma_start(w_stage[:, h % RING, :], d["w_slots"][bass.ds(first_row + h // 2, 1), :, 512 * (h % 2):512 * (h % 2) + 512].rearrange("s p n -> (s p) n")
                          ).then_inc(w_loaded[h % RING], 16)

        def split_hi(act, n, h):
            act.wait_ge(w_loaded[h % RING], n * (2 * SLOTS // RING * 16) + (h // RING + 1) * 16)
            if h % 2 == 0:
                act.wait_ge(slot_used, n * SLOTS + (h // 2 + 1))
            c = slice(512 * (h % 2), 512 * (h % 2) + 512)
            nc.scalar.activation(w_hi[:, h // 2 % RING, c], w_stage[:, h % RING, :], ACT.Copy).then_inc(hi_done, 1)

        def split_lo(pool, n, h):
            pool.wait_ge(hi_done, n * 2 * SLOTS + (h + 1))
            r, c = h // 2 % RING, slice(512 * (h % 2), 512 * (h % 2) + 512)
            pool.tensor_tensor(w_lo[:, r, c], w_stage[:, h % RING, :], w_hi[:, r, c].bitcast(f32), ALU.subtract).then_inc(lo_done, 1)

        def wait_slot(pe, n, j):
            pe.wait_ge(lo_done, n * 2 * SLOTS + (2 * j + 2 + RING))

        def blocks(eng, l, body):
            for kind in range(2):
                with eng.Fori(kind, kind + 1) as b:
                    body(l * NBLK + b, l * SLOTS, kind)
            with eng.Fori(2, NBLK) as b:
                body(l * NBLK + b, (l + b - 2) * SLOTS, 2)

        def wait_bank(eng, n, u, j):
            if j < 3:
                eng.wait_ge(proj.sem, proj.at(n, 3 * u + j + 1))
            else:
                eng.wait_ge(slot_used, n * SLOTS + (4 * u + 5 + RING))

        def stats_steps(vec, buf, count, n, what):
            for t in range(TPB):
                for s in range(2):
                    i = vec.bn_stats(xbn[:, t, 6 * s:6 * s + 6], buf[:, t, 512 * s:512 * s + 512])
            i.then_inc(count.sem, 1)
            vec.wait_ge(count.sem, count.at(n, 1))
            apart()
            for t in range(TPB):
                i = vec.bn_aggr(xagg[:, t, :], xbn[:, t, :])
            i.then_inc(count.sem, 1)
            vec.wait_ge(count.sem, count.at(n, 2))
            vec.tensor_tensor(xms[:, :], xagg[:, :, 0], xagg[:, :, 0], ALU.mult).then_inc(count.sem, 1)
            vec.wait_ge(count.sem, count.at(n, 3))
            vec.scalar_tensor_tensor(xvar[:, :], xms[:, :], EPS, xagg[:, :, 1], ALU.add, ALU.add).then_inc(count.sem, 1)

        def next_norm(vec, m):
            vec.wait_ge(x_in.sem, x_in.at(m, 16))
            stats_steps(vec, xn, xstat, m, "x")
            vec.wait_ge(rstd_x.sem, rstd_x.at(m, 1))
            for t in range(TPB):
                i = vec.tensor_scalar(xn[:, t, :], xn[:, t, :], xrs[:, t:t + 1], None, ALU.mult)
            i.then_inc(xn_sb.sem, 1)

        def next_hi(act, m, k):
            if k == 0:
                act.wait_ge(nw_in.sem, nw_in.at(m, 16))
            act.wait_ge(ht_ps.sem, ht_ps.at(m, k + 1))
            nc.scalar.activation(h_hi[:, k, :], (X if k % 2 == 0 else ATT)[:, :], ACT.Copy, scale=nw[:, k:k + 1]).then_inc(hhi_sb.sem, 1)

        def next_lo(vec, m, k):
            vec.wait_ge(hhi_sb.sem, hhi_sb.at(m, k + 1))
            vec.scalar_tensor_tensor(h_lo[:, k, :], (X if k % 2 == 0 else ATT)[:, :], nw[:, k:k + 1], h_hi[:, k, :].bitcast(f32),
                                     ALU.mult, ALU.subtract).then_inc(hlo_sb.sem, 1)

        def next_transpose(pe, m, k):
            if k == 0:
                pe.wait_ge(xn_sb.sem, xn_sb.at(m, 1))
            dst = X if k % 2 == 0 else ATT
            if k >= 2:
                pe.wait_ge(hlo_sb.sem, hlo_sb.at(m, k - 1))
            for t in range(TPB):
                i = pe.transpose(dst[:, TOK * t:TOK * t + TOK], xn[:, t, 128 * k:128 * k + 128], ident[:, :])
            i.then_inc(ht_ps.sem, 1)

        block = ctx.enter_context(nc.Block())

        @block.sync
        def _(sp):
            def load_next(m):
                src = d["x_prompt"] if m < NBLK or m == DEPTH * NBLK else d["acts"]
                if src is d["acts"]:
                    sp.wait_ge(stored.sem, stored.at(m - NBLK + 1, 0))
                c = m % NBLK * BLK
                sp.dma_start(xn[:, :, :], src[c:c + BLK, :].rearrange("(t p) n -> p t n", p=TOK)).then_inc(x_in.sem, 16)
                sp.dma_start(nw[:, :], d["nw_all"][m, :, :]).then_inc(nw_in.sem, 16)

            def load_par(l):
                sp.dma_start(par[:, :], d["par"][l, :, :]).then_inc(par_in, 16)
                sp.dma_start(w2b[:, :], d["w2b"][l, :, :]).then_inc(par_in, 16)

            def load_states(l, name):
                for i in range(2):
                    sp.dma_start(ss[:, i, :, :], d[name][l * 2 + i, :, :, :]).then_inc(state_in, 16)

            def save_states(l, name):
                for i in range(2):
                    sp.dma_start(d[name][l * 2 + i, :, :, :], ss[:, i, :, :]).then_inc(state_out, 16)

            load_next(0)
            for dst, name in ((ident, "ident"), (xs, "x_sample"), (cum, "cum"), (rmask, "rmask"), (kdec, "kdec"), (qdec, "qdec"),
                              (small, "small"), (comb, "comb"), (ones, "ones")):
                sp.dma_start(dst[:], d[name]).then_inc(const_in, 16)
            load_par(0)
            for n in range(DEPTH * NBLK):
                l, b = n // NBLK, n % NBLK
                if n > 0:
                    sp.wait_ge(rope_st.sem, rope_st.at(n - 1, 18))
                sp.dma_start(rope[:, :, :], d["rope"][b, :, :, :]).then_inc(rope_in.sem, 16)
                if b == 0:
                    sp.wait_ge(s_v.sem, s_v.at(l, 0))
                    load_states(l, "state_ret")
                sp.wait_ge(ht_ps.sem, ht_ps.at(n, 8))
                sp.wait_ge(hlo_sb.sem, hlo_sb.at(n, 8))
                load_next(n + 1)
                if b == 1:
                    sp.wait_ge(s_v.sem, s_v.at(l, V_DEC[0] + 8))
                    save_states(l, "ret_s")
                    sp.wait_ge(state_out, l * 64 + 32)
                    sp.wait_ge(so_ps.sem, so_ps.at(l, 1))
                    load_states(l, "state_gla")
                    sp.wait_ge(s_v.sem, s_v.at(l, V_DEC[1] + 8))
                    save_states(l, "gla_s")
                if b == NBLK - 1 and l < DEPTH - 1:
                    sp.wait_ge(gate_x.sem, gate_x.at(n, 2))
                    sp.wait_ge(s_v.sem, s_v.at(l, V_LAST))
                    load_par(l + 1)
                sp.wait_ge(st_ps.sem, st_ps.at(n, 8))
                src = d["x_prompt"] if l == 0 else d["acts"]
                rows = slice(b * BLK, b * BLK + BLK)
                sp.dma_start(y_t[:, :, :], src[rows, :].rearrange("(t p) n -> p t n", p=TOK)).then_inc(res_in.sem, 16)
                sp.wait_ge(sgla_sb.sem, sgla_sb.at(n, 9))
                sp.dma_start(fin_w, d["fin_w"]).then_inc(fin_in.sem, 16)
                if b == NBLK - 1:
                    sp.wait_ge(sret_sb.sem, sret_sb.at(n, 4))
                    sp.dma_start(d["ret_p"][l, :, :], s_ret[:, :]).then_inc(st_saved, 16)
                    sp.wait_ge(sgla_sb.sem, sgla_sb.at(n, 9))
                    sp.dma_start(d["gla_p"][l, :, :], s_gla[:, :]).then_inc(st_saved, 16)
                sp.wait_ge(y_add.sem, y_add.at(n, 8))
                sp.wait_ge(yn_sb.sem, yn_sb.at(n, 1))
                if l < DEPTH - 1:
                    dst, out = d["acts"], y_t
                else:
                    dst, out = d["y_prompt"], yn
                sp.dma_start(dst[rows, :].rearrange("(t p) n -> p t n", p=TOK), out[:, :, :]).then_inc(stored.sem, 16)
                if n == (DEPTH - 1) * NBLK + 1:
                    sp.wait_ge(s_v.sem, s_v.at(l, V_LAST))
                    sp.wait_ge(state_out, l * 64 + 64)
                    sp.dma_start(d["y_sample"], ys).then_inc(fin_out, 16)
            sp.wait_ge(x_in.sem, x_in.at(DEPTH * NBLK, 16))
            sp.wait_ge(nw_in.sem, nw_in.at(DEPTH * NBLK, 16))
            sp.wait_ge(fin_out, 16)
            sp.wait_ge(st_saved, 16 * 2 * DEPTH + 32)
            sp.wait_ge(state_out, 16 * 4 * DEPTH)
            sp.wait_ge(stored.sem, stored.at(DEPTH * NBLK, 0))

        @block.gpsimd
        def _(pool):
            pool.memset(half[:, :], -0.5).then_inc(sets, 1)
            pool.memset(lr_s[:, :], 1.0).then_inc(sets, 1)
            pool.memset(a_gla[:, :, :], 0.0).then_inc(sets, 1)
            for c, (s, credit) in enumerate(((lo_done, RING), (slot_used, RING), (stored.sem, 16), (y_add.sem, 8), (st_saved, 32))):
                pool.memset(tmp[:, 0, c:c + 1], 0.0).then_inc(s, credit)
            pool.wait_ge(sets, 3)

            def rsqrt(dst, src, s):
                pool.tensor_tensor(dst, src, half[0:dst.shape[0], 0:dst.shape[-1]], ALU.pow).then_inc(s, 1)

            pool.wait_ge(s_v.sem, s_v.at(0, 4 - 6))
            rsqrt(srs[:, :], svar[:, :], s_p.sem)
            pool.wait_ge(xstat.sem, xstat.at(0, 4))
            rsqrt(xrs[:, :], xvar[:, :], rstd_x.sem)
            for h in range(2 * AHEAD):
                split_lo(pool, 0, h)

            with pool.Fori(0, DEPTH) as l:
                def body(n, next_row, kind):
                    for w in range(SLOTS):
                        split_lo(pool, n, 2 * (w + AHEAD))
                        split_lo(pool, n, 2 * (w + AHEAD) + 1)
                        for g, first in ((0, 10), (1, 22)):
                            t = w - first
                            if 0 <= t < TPB:
                                pool.wait_ge(ostat.sem, ostat.at(n, 3 * (t + 1) if g == 0 else 12 + 4 * (t + 1)))
                                rsqrt(rstd[:, t % 2, :], var[:, t % 2, :], rstd_o.sem)
                        if w == 19:
                            pool.wait_ge(xstat.sem, xstat.at(n + 1, 4))
                            rsqrt(xrs[:, :], xvar[:, :], rstd_x.sem)
                        if w == 23 and kind == 1:
                            pool.wait_ge(s_v.sem, s_v.at(l, V_VAR))
                            rsqrt(rs_s[:, :], v_s[:, 0, :], s_p.sem)
                        for i, c in enumerate(MIX_ORDER):
                            if w == c:
                                pool.wait_ge(mhi_sb.sem, mhi_sb.at(n, i + 1))
                                g, t = (4, i) if i < 4 else (0, i - 4)
                                pool.tensor_tensor(m_lo[:, g:g + 4, TOK * t:TOK * t + TOK], tmp[:, t % 2, :].rearrange("p (h n) -> p h n", h=4),
                                                   m_hi[:, g:g + 4, TOK * t:TOK * t + TOK].bitcast(f32), ALU.subtract).then_inc(mlo_sb.sem, 1)
                    pool.wait_ge(ystat.sem, ystat.at(n, 4))
                    rsqrt(yrs[:, :], xvar[:, :], rstd_y.sem)
                    if kind == 1:
                        pool.wait_ge(s_v.sem, s_v.at(l, V_NV))
                        rsqrt(srs[:, :], svar[:, :], s_p.sem)

                blocks(pool, l, body)

        @block.tensor
        def _(pe):
            pe.wait_ge(const_in, 144)

            for k in range(KT):
                next_transpose(pe, 0, k)
            with pe.Fori(0, DEPTH) as l:
                def body(n, next_row, kind):
                    def hT_slot0():
                        pe.wait_ge(hlo_sb.sem, hlo_sb.at(n, 8))
                        if kind == 0:
                            pe.wait_ge(s_v.sem, s_v.at(l, 0))
                            for k in range(KT):
                                i = pe.matmul(X[:, 8 * k:8 * k + 8], xsn[:, 128 * k:128 * k + 128], ident[0:8, 0:8], start=True, stop=True)
                            i.then_inc(xs_t.sem, 1)
                        wait_slot(pe, n, 0)
                        prods = [(w_hi, h_hi), (w_hi, h_lo), (w_lo, h_hi)]
                        for k in range(KT):
                            for c, (w, h) in enumerate(prods):
                                i = pe.matmul(ATT[:, :], w[:, 0, 128 * k:128 * k + 128], h[:, k, :], start=(k == 0 and c == 0), stop=(k == KT - 1 and c == 2))
                        if kind == 0:
                            pe.wait_ge(s_v.sem, s_v.at(l, V_H))
                            for k in range(KT):
                                for part in (w_hi, w_lo):
                                    i = pe.matmul(X[0:16, 256:384], hs[:, k, :], part[:, 0, 128 * k:128 * k + 128],
                                                  start=(k == 0 and part is w_hi), stop=(k == KT - 1 and part is w_lo))
                        i.then_inc(slot_used, 1)

                    def unit_slot(u, s):
                        j = 1 + 4 * u + s
                        wait_slot(pe, n, j)
                        r = j % RING
                        natural = u in (1, 4, 6, 7)
                        for q in range(4):
                            if s == 0:
                                free_bank(u, q)
                            for kk in range(2):
                                k = 2 * s + kk
                                if u >= 6:
                                    k = (k + 4) % 8
                                a_hi, a_lo = (m_hi, m_lo) if u >= 6 else (h_hi, h_lo)
                                if natural:
                                    cols = slice(512 * kk, 512 * kk + 512)
                                    tile = slice(TOK * q, TOK * q + TOK)
                                    prods = [(a_hi[:, k, tile], w_hi[:, r, cols]), (a_hi[:, k, tile], w_lo[:, r, cols]), (a_lo[:, k, tile], w_hi[:, r, cols])]
                                else:
                                    cols = slice(512 * kk + 128 * q, 512 * kk + 128 * q + 128)
                                    prods = [(w_hi[:, r, cols], a_hi[:, k, :]), (w_hi[:, r, cols], a_lo[:, k, :]), (w_lo[:, r, cols], a_hi[:, k, :])]
                                for c, (x, y) in enumerate(prods):
                                    i = pe.matmul(P[q][:, :], x, y, start=(s == 0 and kk == 0 and c == 0), stop=(s == 3 and kk == 1 and c == 2),
                                                  skip_group_check=True)
                            if q < 3 and s == 3:
                                i.then_inc(proj.sem, 1)
                        if kind == 0 and u < 6:
                            if s == 0:
                                free_sample_bank(u)
                            for kk in range(2):
                                for part in (w_hi, w_lo):
                                    i = pe.matmul((ST if Z_BANK[u] == "S" else X)[0:16, :], hs[:, 2 * s + kk, :], part[:, r, 512 * kk:512 * kk + 512],
                                                  start=(s == 0 and kk == 0 and part is w_hi), stop=(s == 3 and kk == 1 and part is w_lo))
                        if kind == 1 and u >= 6:
                            if u == 6 and s == 0:
                                pe.wait_ge(s_v.sem, s_v.at(l, V_MIX))
                                pe.wait_ge(o_sb.sem, o_sb.at(n, 8))
                            if u == 7 and s == 0:
                                pe.wait_ge(s_v.sem, s_v.at(l, V_X0))
                            for kk in range(2):
                                k = (2 * s + kk + 4) % 8
                                for c, (m, part) in enumerate(((ms[:, k, 0:8], w_hi), (ms[:, k, 0:8], w_lo), (ms[:, k, 8:16], w_hi))):
                                    i = pe.matmul(OB[0:8, :], m, part[:, r, 512 * kk:512 * kk + 512],
                                                  start=(s == 0 and kk == 0 and c == 0), stop=(s == 3 and kk == 1 and c == 2))
                        i.then_inc(slot_used, 1)

                    def free_sample_bank(u):
                        if u == 1:
                            pe.wait_ge(z_sb.sem, z_sb.at(l, 2))
                        elif u == 2:
                            pe.wait_ge(kn_sb.sem, kn_sb.at(n, 2))
                        elif u == 3:
                            pe.wait_ge(sret_sb.sem, sret_sb.at(n, 4))
                        elif u == 4:
                            pe.wait_ge(z_sb.sem, z_sb.at(l, 5))
                        elif u == 5:
                            pe.wait_ge(kn_sb.sem, kn_sb.at(n, 4))

                    def z_transposed(c, dst, columns, what):
                        pe.wait_ge(z_sb.sem, z_sb.at(l, what))
                        for q in range(columns):
                            i = pe.matmul(dst[:, c + 8 * q:c + 8 * q + 8], z_u[0:16, 128 * q:128 * q + 128], comb[:, 0:8], start=True, stop=True)
                        i.then_inc(zt_ps.sem, 1)

                    def sample_outputs(g):
                        pe.wait_ge(kn_sb.sem, kn_sb.at(n, 2 + 2 * g))
                        for p in range(2):
                            for t in range(DECB):
                                c = 2 * (8 * p + t)
                                i = pe.matmul(X[:, c:c + 2], ss[:, p, t, :], q_s[:, g, p, t, :], start=True, stop=True)
                        i.then_inc(so_ps.sem, 1)

                    def sample_work(w):
                        if kind == 0:
                            if w == 1:
                                z_transposed(128, X, 1, 1)
                            if w == 2:
                                pe.wait_ge(zt_sb.sem, zt_sb.at(l, 1))
                                for q in range(2):
                                    i = pe.matmul(X[:, 144 + 8 * q:152 + 8 * q], w2b[0:RANK + 1, 128 * q:128 * q + 128], lr_s[0:RANK + 1, 0:8], start=True, stop=True)
                                i.then_inc(gx_ps.sem, 1)
                            if w == 6:
                                pe.wait_ge(em_sb.sem, em_sb.at(n, 1))
                                z_transposed(128, X, 4, 2)
                            if w == 13:
                                z_transposed(0, ATT, 4, 4)
                            if w == 17:
                                pe.wait_ge(zt_sb.sem, zt_sb.at(l, 3))
                                z_transposed(0, ATT, 4, 5)
                            if w == 25:
                                z_transposed(0, ATT, 4, 7)
                        if kind == 1:
                            if w in V_AT:
                                c = V_AT.index(w)
                                if c in (1, 2, 3, 4, 5, 6, 7):
                                    pe.wait_ge(s_v.sem, s_v.at(l, V_DEC[0] + c))
                                if c == 8:
                                    pe.wait_ge(s_v.sem, s_v.at(l, V_O[0]))
                                if c > 8:
                                    pe.wait_ge(s_v.sem, s_v.at(l, V_DEC[1] + c - 8))
                                if c == 10:
                                    pe.wait_ge(sret_sb.sem, sret_sb.at(n, 4))
                                i = pe.matmul((X if w in (11, 12) else ST)[:, :], comb[:, c % 8:c % 8 + 1].to_broadcast([16, 128]), z_v[:, c // 8, :], start=True, stop=True)
                                i.then_inc(vb_ps.sem, 1)
                            if w == 9:
                                sample_outputs(0)
                            if w == 21:
                                sample_outputs(1)
                            if w == 22:
                                pe.wait_ge(s_v.sem, s_v.at(l, V_SQ))
                                pe.matmul(X[:, 128:256], ones[:, :], o_s[:, :, :].rearrange("p a n -> p (a n)"), start=True, stop=True).then_inc(mom_ps.sem, 1)

                    def free_bank(u, q):
                        if u == 0:
                            pe.wait_ge(y_add.sem, n * 8 + (4 + q + 1))
                        elif u == 1:
                            pe.wait_ge(q_raw.sem, q_raw.at(n, q + 1)) if q < 2 else pe.wait_ge(k_raw.sem, k_raw.at(n, q - 1))
                        elif u == 2:
                            pe.wait_ge(v_sb.sem, v_sb.at(n, q + 1))
                        elif u == 3:
                            pe.wait_ge(g_silu.sem, g_silu.at(n, q + 1))
                        elif u == 4:
                            pe.wait_ge(qk_gla.sem, qk_gla.at(n, q + 1))
                        elif u == 5:
                            pe.wait_ge(v_sb.sem, v_sb.at(n, 4 + q + 1))
                        elif u == 6:
                            pe.wait_ge(g_silu.sem, g_silu.at(n, 4 + q + 1))
                        else:
                            pe.wait_ge(y_add.sem, y_add.at(n, q + 1))

                    def keys_natural(g):
                        if g == 0:
                            pe.wait_ge(rope_st.sem, rope_st.at(n, 8))
                            pe.wait_ge(ex_sb.sem, ex_sb.at(n, 2))
                            pe.wait_ge(em_sb.sem, em_sb.at(n, 1))
                            if kind == 0:
                                pe.wait_ge(zt_sb.sem, zt_sb.at(l, 2))
                        else:
                            pe.wait_ge(qk_gla.sem, qk_gla.at(n, 4))
                            pe.wait_ge(m_aff.sem, m_aff.at(n, 4))
                            pe.wait_ge(att_sb.sem, att_sb.at(n, 4))
                            if kind == 0:
                                pe.wait_ge(zt_sb.sem, zt_sb.at(l, 4))
                        for t in range(TPB):
                            for p in range(2):
                                c = 256 * (t % 2) + 128 * p
                                i = pe.transpose((X, ATT)[t // 2][:, c:c + 128], k_t[:, p, TOK * t:TOK * t + TOK], ident[:, :])
                            if t % 2 == 1:
                                i.then_inc(kn_ps.sem, 1)

                    def scores(g, t):
                        tile = slice(TOK * t, TOK * t + TOK)
                        if g == 0 and t == 0:
                            pe.wait_ge(rope_st.sem, rope_st.at(n, 18))
                        if t == 0:
                            pe.wait_ge(kn_sb.sem, kn_sb.at(n, 2 * g + 2))
                        else:
                            pe.wait_ge(att_sb.sem, att_sb.at(n, 4 * g + t))
                        for p in range(2):
                            for hh in range(2):
                                h = 2 * p + hh
                                i = pe.matmul(ATT[:, 128 * h:128 * h + 128], k_t[:, p, tile], q_t[:, p, hh, tile], start=True, stop=True)
                        i.then_inc(att_ps.sem, 1)

                    def outputs(g, t):
                        tile = slice(TOK * t, TOK * t + TOK)
                        a, s = (a_ret, s_ret) if g == 0 else (a_gla, s_mid)
                        pe.wait_ge(att_sb.sem, att_sb.at(n, 4 * g + t + 1))
                        pe.wait_ge(v_sb.sem, v_sb.at(n, 4 * g + t + 1))
                        if g == 0 and t == 0:
                            pe.wait_ge(ex_sb.sem, ex_sb.at(n, 4))
                        if t == 0 and kind == 0:
                            pe.wait_ge(z_sb.sem, z_sb.at(l, 6 if g else 3))
                        if t == 0 and kind == 1:
                            pe.wait_ge(s_v.sem, s_v.at(l, V_DEC[g] + 8))
                        if g + t > 0:
                            pe.wait_ge(o_sb.sem, o_sb.at(n, 4 * g + t))
                        if g == 0 and t > 0:
                            pe.wait_ge(sret_sb.sem, sret_sb.at(n, t))
                        if g == 1:
                            pe.wait_ge(sret_sb.sem, sret_sb.at(n, 4))
                            pe.wait_ge(sgla_sb.sem, sgla_sb.at(n, 1 + 2 * t))
                        for h in range(HEADS):
                            hc = slice(128 * h, 128 * h + 128)
                            pe.matmul(OB[:, hc], a[:, h, :], v_n[:, t, hc], start=True, stop=False)
                            i = pe.matmul(OB[:, hc], q_t[:, h // 2, h % 2, tile], s[:, hc], start=False, stop=True)
                        i.then_inc(o_ps.sem, 1)
                        for p in range(2):
                            i = pe.matmul(ST[:, 256 * p:256 * p + 256], k_n[:, t, 128 * p:128 * p + 128], v_n[:, t, 256 * p:256 * p + 256], start=True, stop=True)
                        i.then_inc(st_ps.sem, 1)

                    def mixed_t(g, t):
                        pe.wait_ge(normed.sem, normed.at(n, 4 * g + t + 1))
                        dst = X if g == 0 or t % 2 == 0 else ST
                        if g == 0:
                            pe.wait_ge(kn_sb.sem, kn_sb.at(n, 2)) if t == 0 else pe.wait_ge(m_aff.sem, m_aff.at(n, t))
                            if kind == 0:
                                pe.wait_ge(z_sb.sem, z_sb.at(l, 4))
                            if kind == 1:
                                pe.wait_ge(s_v.sem, s_v.at(l, V_DEC[1] + 2))
                        elif t < 2:
                            pe.wait_ge(kn_sb.sem, kn_sb.at(n, 4))
                            pe.wait_ge(sgla_sb.sem, sgla_sb.at(n, 8))
                            if kind == 0:
                                pe.wait_ge(z_sb.sem, z_sb.at(l, 7))
                            if kind == 1:
                                pe.wait_ge(s_v.sem, s_v.at(l, V_MOM))
                        else:
                            pe.wait_ge(mix_sb.sem, mix_sb.at(n, 4 + t - 1))
                        for h in range(HEADS):
                            i = pe.transpose(dst[:, 128 * h:128 * h + 128], o_n[:, t, 128 * h:128 * h + 128], ident[:, :])
                        i.then_inc(mt_ps.sem, 1)

                    hT_slot0()
                    sample_work(0)
                    for w in range(1, SLOTS):
                        u, s = (w - 1) // 4, (w - 1) % 4
                        if u == 6 and s == 0:
                            pe.wait_ge(mlo_sb.sem, mlo_sb.at(n, 4))
                        if u == 6 and s == 2:
                            pe.wait_ge(mlo_sb.sem, mlo_sb.at(n, 8))
                        unit_slot(u, s)
                        if w == 1:
                            for hf, dst in ((0, ATT), (1, OB)):
                                if hf == 0:
                                    pe.wait_ge(lr_sb.sem, lr_sb.at(n, 1))
                                elif kind == 2:
                                    pe.wait_ge(s_v.sem, s_v.at(l, V_X1))
                                for t2 in range(2):
                                    t = 2 * hf + t2
                                    i = pe.matmul(dst[:, 256 * t2:256 * t2 + 256], lr_t[0:RANK + 1, TOK * t:TOK * t + TOK], w2b[:, :], start=True, stop=True)
                                i.then_inc(gate_x.sem, 1)
                        if w == 4:
                            for p, dst in ((0, ATT), (1, OB)):
                                pe.wait_ge(la_sb.sem, la_sb.at(n, 2))
                                for t in range(TPB):
                                    i = pe.matmul(dst[:, TOK * t:TOK * t + TOK], la[:, t, 128 * p:128 * p + 128], cum[:, 0:128], start=True, stop=True)
                                i.then_inc(cum_b.sem, 1)
                            if kind == 0:
                                pe.wait_ge(s_v.sem, s_v.at(l, V_LA))
                            for t in range(TPB):
                                for p in range(2):
                                    c = 4 * t + 2 * p
                                    i = pe.matmul(X[:, c:c + 2], la[:, t, 128 * p:128 * p + 128], cum[:, 128:130], start=True, stop=True)
                            i.then_inc(mid_b.sem, 1)
                        if w in (7, 19):
                            keys_natural(w // 19)
                        for g, first in ((0, 8), (1, 20)):
                            t = w - first
                            if 1 <= t <= TPB:
                                outputs(g, t - 1)
                            if 0 <= t < TPB:
                                scores(g, t)
                        if 13 <= w < 17:
                            mixed_t(0, w - 13)
                        if w in (25, 26):
                            mixed_t(1, 2 * (w - 25))
                            mixed_t(1, 2 * (w - 25) + 1)
                        if 27 <= w < 31:
                            for k in (2 * (w - 27), 2 * (w - 27) + 1):
                                if k == 0:
                                    pe.wait_ge(mix_sb.sem, mix_sb.at(n, 7))
                                if k == 1:
                                    pe.wait_ge(att_sb.sem, att_sb.at(n, 8))
                                    if kind == 0:
                                        pe.wait_ge(zt_sb.sem, zt_sb.at(l, 5))
                                next_transpose(pe, n + 1, k)
                        sample_work(w)

                blocks(pe, l, body)

        @block.scalar
        def _(act):
            act.wait_ge(sets, 3)
            load_half(act, 0, 0, 0)
            load_half(act, 0, 0, 1)
            for h in range(2 * AHEAD):
                split_hi(act, 0, h)
                load_half(act, 0, 0, h + 2)
            for k in range(KT):
                next_hi(act, 0, k)
            with act.Fori(0, DEPTH) as l:
                def body(n, next_row, kind):
                    def z_out(w):
                        u = Z_READ.index(w)
                        if u in (2, 3, 5):
                            act.wait_ge(zt_ps.sem, zt_ps.at(l, {2: 2, 3: 3, 5: 4}[u]))
                        elif u == 0:
                            act.wait_ge(zt_ps.sem, zt_ps.at(l, 1))
                        act.wait_ge(slot_used, n * SLOTS + (w + RING))
                        dst = z_v[:, u // 4, :] if u in (1, 4) else z_u[:, :]
                        nc.scalar.activation(dst, (ST if Z_BANK[u] == "S" else X)[0:16, :], ACT.Copy).then_inc(z_sb.sem, 1)

                    def sample_work(w):
                        if kind == 1 or kind == 2:
                            return
                        if w == 1:
                            act.wait_ge(slot_used, n * SLOTS + (1 + RING))
                            nc.scalar.activation(z_u[:, 0:128], X[0:16, 256:384], ACT.Copy).then_inc(z_sb.sem, 1)
                        if w == 2:
                            act.wait_ge(zt_ps.sem, zt_ps.at(l, 1))
                            nc.scalar.activation(lr_s[0:16, :], X[0:16, 128:136], ACT.Copy).then_inc(zt_sb.sem, 1)
                        if w == 3:
                            act.wait_ge(gx_ps.sem, gx_ps.at(l, 1))
                            nc.scalar.activation(gt[:, :], X[:, 144:160], ACT.Abs).then_inc(gl_s.sem, 1)
                            act.wait_ge(gl_s.sem, gl_s.at(l, 1))
                            nc.scalar.activation(gt[:, :], gt[:, :], ACT.Exp, scale=-1.0).then_inc(gl_s.sem, 1)
                            act.wait_ge(gl_s.sem, gl_s.at(l, 2))
                            nc.scalar.activation(gt[:, :], gt[:, :], ACT.Ln, bias=1.0).then_inc(gl_s.sem, 1)
                        if w in (7, 14, 18, 26):
                            c = (7, 14, 18, 26).index(w)
                            act.wait_ge(zt_ps.sem, zt_ps.at(l, c + 2))
                            nc.scalar.activation(z_t[:, 4 * c:4 * c + 4, :], (X[:, 128:160] if c == 0 else ATT[:, 0:32]).rearrange("p (a b) -> p a b", b=8),
                                                 ACT.Copy).then_inc(zt_sb.sem, 1)
                        if w == 7:
                            act.wait_ge(s_v.sem, s_v.at(l, V_LA))
                            nc.scalar.activation(al[:, :], al[:, :], ACT.Exp, scale=1.0 / TAU).then_inc(al_s.sem, 1)
                        if w == 27:
                            act.wait_ge(zt_sb.sem, zt_sb.at(l, 5))
                            for g in range(2):
                                nc.scalar.activation(sg_s[:, 32 * g:32 * g + 32].rearrange("p (a b) -> p a b", b=8), z_t[:, 4 + 8 * g:8 + 8 * g, :],
                                                     ACT.Tanh, scale=0.5).then_inc(tg_s.sem, 1)

                    for w in range(SLOTS):
                        if w == 5:
                            for q in range(2):
                                if q == 0:
                                    act.wait_ge(stored.sem, stored.at(n, 0))
                                wait_bank(act, n, 0, 2 + q)
                                nc.scalar.activation(k_t[:, q, :], P[2 + q][:, :], ACT.Copy).then_inc(k_raw.sem, 1)
                        if w in (9, 21):
                            g = w // 21
                            for q in range(4):
                                wait_bank(act, n, 1 + 3 * g, q)
                                nc.scalar.activation(v_n[:, q, :], P[q][:, :], ACT.Copy).then_inc(v_sb.sem, 1)
                        if w in (13, 25):
                            g = w // 25
                            if g == 1:
                                act.wait_ge(mix_sb.sem, mix_sb.at(n, 4))
                            for q in range(4):
                                wait_bank(act, n, 2 + 3 * g, q)
                                nc.scalar.activation(g_t[:, q, :], P[q][:, :], ACT.Tanh, scale=0.5).then_inc(g_tanh.sem, 1)
                        if kind == 0 and w in Z_READ:
                            z_out(w)
                        for h in (2 * (w + AHEAD), 2 * (w + AHEAD) + 1):
                            split_hi(act, n, h)
                            load_half(act, l * SLOTS if h + 2 < 2 * SLOTS else next_row - SLOTS, n, h + 2)
                        sample_work(w)
                        if w == 1:
                            act.wait_ge(slot_used, n * SLOTS + (1 + RING))
                            act.wait_ge(lr_ones.sem, lr_ones.at(n, 1))
                            nc.scalar.activation(lr_t[0:RANK, :], ATT[0:RANK, :], ACT.Copy).then_inc(lr_sb.sem, 1)
                        if w == 2:
                            for hf, src in ((0, ATT), (1, OB)):
                                act.wait_ge(gate_x.sem, gate_x.at(n, hf + 1))
                                nc.scalar.activation(tmp[:, hf, :], src[:, :], ACT.Abs).then_inc(gate_l.sem, 1)
                                act.wait_ge(gate_l.sem, gate_l.at(n, 3 * hf + 1))
                                nc.scalar.activation(tmp[:, hf, :], tmp[:, hf, :], ACT.Exp, scale=-1.0).then_inc(gate_l.sem, 1)
                                act.wait_ge(gate_l.sem, gate_l.at(n, 3 * hf + 2))
                                nc.scalar.activation(tmp[:, hf, :], tmp[:, hf, :], ACT.Ln, bias=1.0).then_inc(gate_l.sem, 1)
                        if w == 6:
                            for p, src in ((0, ATT), (1, OB)):
                                act.wait_ge(cum_b.sem, cum_b.at(n, p + 1))
                                for sgn in range(2):
                                    nc.scalar.activation(ex[:, p, sgn, :], src[:, :], ACT.Exp, scale=1.0 - 2.0 * sgn).then_inc(ex_sb.sem, 1)
                            act.wait_ge(mid_b.sem, mid_b.at(n, 1))
                            nc.scalar.activation(em[:, :, :, :].rearrange("p a b c -> p (a b c)"), X[:, 0:16], ACT.Exp).then_inc(em_sb.sem, 1)
                        for g, first in ((0, 10), (1, 22)):
                            t = w - first
                            if 0 <= t < TPB:
                                act.wait_ge(o_ps.sem, o_ps.at(n, 4 * g + t + 1))
                                nc.scalar.activation(o_n[:, t, :], OB[:, :], ACT.Copy).then_inc(o_sb.sem, 1)
                        if 14 <= w < 18:
                            t = w - 14
                            act.wait_ge(mt_ps.sem, mt_ps.at(n, t + 1))
                            if t >= 2:
                                act.wait_ge(mlo_sb.sem, mlo_sb.at(n, t - 1))
                            for h in range(HEADS):
                                i = nc.scalar.activation(tmp[:, t % 2, 128 * h:128 * h + 128], X[:, 128 * h:128 * h + 128], ACT.Identity,
                                                         scale=parh[:, 1 + h:2 + h], bias=parh[:, 5 + h:6 + h])
                            i.then_inc(m_aff.sem, 1)
                        for i_, c in enumerate(MIX_ORDER):
                            if w == c:
                                act.wait_ge(mix_sb.sem, mix_sb.at(n, i_ + 1))
                                g, t = (4, i_) if i_ < 4 else (0, i_ - 4)
                                nc.scalar.activation(m_hi[:, g:g + 4, TOK * t:TOK * t + TOK], tmp[:, t % 2, :].rearrange("p (h n) -> p h n", h=4), ACT.Copy).then_inc(mhi_sb.sem, 1)
                        if 28 <= w < 32:
                            next_hi(act, n + 1, 2 * (w - 28))
                            next_hi(act, n + 1, 2 * (w - 28) + 1)
                blocks(act, l, body)
            for h in (2 * (SLOTS + AHEAD), 2 * (SLOTS + AHEAD) + 1):
                act.wait_ge(w_loaded[h % RING], (DEPTH * NBLK - 1) * (2 * SLOTS // RING * 16) + (h // RING + 1) * 16)

        @block.vector
        def _(vec):
            vec.wait_ge(const_in, 144)
            vec.wait_ge(sets, 3)

            def step(i):
                i.then_inc(s_v.sem, 1)

            def sample_norm(l, k):
                for s in range(2):
                    i = vec.bn_stats(sbn[:, 6 * s:6 * s + 6], xs[:, 512 * s:512 * s + 512])
                step(i)
                vec.wait_ge(s_v.sem, s_v.at(l, k + 1))
                apart()
                step(vec.bn_aggr(sagg[:, :], sbn[:, :]))
                vec.wait_ge(s_v.sem, s_v.at(l, k + 2))
                step(vec.tensor_tensor(smsq[:, :], sagg[:, 0:1], sagg[:, 0:1], ALU.mult))
                vec.wait_ge(s_v.sem, s_v.at(l, k + 3))
                step(vec.scalar_tensor_tensor(svar[:, :], smsq[:, :], EPS, sagg[:, 1:2], ALU.add, ALU.add))
                if k < 0:
                    vec.wait_ge(s_p.sem, s_p.at(l, 0))
                else:
                    vec.wait_ge(s_p.sem, s_p.at(l, 2))
                    vec.wait_ge(state_out, l * 64 + 64)
                step(vec.tensor_scalar(xsn[:, :], xs[:, :], srs[:, :], None, ALU.mult))
                if k < 0:
                    i = vec.memset(spare[:, 63:64], 0.0)
                else:
                    i = vec.scalar_tensor_tensor(ys[:, :], xs[:, :], srs[:, :], fin_w[0:8, :], ALU.mult, ALU.mult)
                step(i)

            vec.tensor_scalar(gmask[:, :], rmask[:, 0:TOK], 0.0, None, ALU.is_gt)
            vec.memset(lr_t, 1.0).then_inc(lr_ones.sem, 1)
            sample_norm(0, -6)
            next_norm(vec, 0)
            for k in range(KT):
                next_lo(vec, 0, k)
            with vec.Fori(0, DEPTH) as l:
                def body(n, next_row, kind):
                    def done(k):
                        vec.wait_ge(s_v.sem, s_v.at(l, k))

                    def sample_start():
                        vec.wait_ge(st_saved, l * 32 + 32)
                        vec.memset(s_ret[:, :], 0.0)
                        vec.memset(s_gla[:, :], 0.0)
                        vec.wait_ge(par_in, l * 32 + 32)
                        vec.wait_ge(xs_t.sem, xs_t.at(l, 1))
                        hs_v = hs_f[:, :].rearrange("p (k b) -> p k b", b=8)
                        step(vec.tensor_tensor(hs_v, X[:, 0:64].rearrange("p (k b) -> p k b", b=8),
                                               par[:, 0:8].unsqueeze(2).to_broadcast([128, 8, 8]), ALU.mult))
                        done(1)
                        step(vec.tensor_copy(hs[:, :, 0:8], hs_v))
                        done(2)
                        step(vec.tensor_tensor(hs[:, :, 8:16], hs_v, hs[:, :, 0:8].bitcast(f32), ALU.subtract))
                        vec.tensor_scalar(parh[:, :], par[:, 8:17], 0.5, None, ALU.mult)

                    def sample_gate():
                        vec.wait_ge(gl_s.sem, gl_s.at(l, 3))
                        step(vec.scalar_tensor_tensor(al[:, :], X[:, 144:160], 0.0, gt[:, :], ALU.min, ALU.subtract))

                    def sample_q_ret():
                        vec.wait_ge(zt_sb.sem, zt_sb.at(l, 2))
                        step(vec.memset(q_s[:, :, :, :, :], 0.0))
                        done(5)
                        apart()
                        step(vec.stream_shuffle(rot[:, :, :], z_t[:, 0:4, :], [(p + 16) % 32 for p in range(32)]))
                        done(6)
                        vec.tensor_scalar(z_t[:, 0:2, :], z_t[:, 0:2, :], small[:, 0:1], None, ALU.mult)
                        step(vec.tensor_scalar(z_t[:, 2:4, :], z_t[:, 2:4, :], small[:, 2:3], None, ALU.mult))
                        done(7)
                        vec.scalar_tensor_tensor(rot[:, 0:2, :], rot[:, 0:2, :], small[:, 1:2], z_t[:, 0:2, :], ALU.mult, ALU.add)
                        step(vec.scalar_tensor_tensor(rot[:, 2:4, :], rot[:, 2:4, :], small[:, 3:4], z_t[:, 2:4, :], ALU.mult, ALU.add))
                        done(8)
                        for hh in range(2):
                            r = slice(64 * hh, 64 * hh + 64)
                            vec.tensor_copy(q_s[r, 0, :, :, hh], rot[r, 0:2, :])
                        step(vec.tensor_copy(k_s[:, 0, :, :], rot[:, 2:4, :]))

                    def sample_q_gla():
                        vec.wait_ge(zt_sb.sem, zt_sb.at(l, 4))
                        for hh in range(2):
                            r = slice(64 * hh, 64 * hh + 64)
                            vec.tensor_scalar(q_s[r, 1, :, :, hh], z_t[r, 8:10, :], DK ** -0.5, None, ALU.mult)
                        step(vec.tensor_copy(k_s[:, 1, :, :], z_t[:, 10:12, :]))

                    def sample_decay(g):
                        vec.wait_ge(state_in, l * 64 + 32 * g + 32)
                        if g == 0:
                            for p in range(2):
                                i = vec.tensor_scalar(ss[:, p, :, :], ss[:, p, :, :], small[:, 4 + p:5 + p], None, ALU.mult)
                            step(i)
                        else:
                            vec.wait_ge(al_s.sem, al_s.at(l, 1))
                            s2 = ss[:, :, :, :].rearrange("p i b n -> p (i b) n")
                            step(vec.tensor_tensor(s2, s2, al[:, :].unsqueeze(2).to_broadcast([128, 16, 128]), ALU.mult))

                    def sample_update(c):
                        g, t = c // DECB, c % DECB
                        if t == 0:
                            done(V_DEC[g])
                        vec.wait_ge(vb_ps.sem, vb_ps.at(l, c + 1))
                        src = X if V_AT[c] in (11, 12) else ST
                        for p in range(2):
                            for hh in range(2):
                                r, h = slice(64 * hh, 64 * hh + 64), 2 * p + hh
                                i = vec.scalar_tensor_tensor(ss[r, p, t, :], src[r, 128 * h:128 * h + 128], k_s[r, g, p, t:t + 1], ss[r, p, t, :], ALU.mult, ALU.add)
                        step(i)

                    def sample_o(g):
                        vec.wait_ge(so_ps.sem, so_ps.at(l, g + 1))
                        for hh in range(2):
                            i = vec.tensor_copy(o_s[:, 0, 32 * g:32 * g + 32].rearrange("p (a h b) -> p a h b", a=2, h=2)[:, :, hh, :],
                                                X[:, 0:32].rearrange("p (a b h) -> p a b h", a=2, h=2)[:, :, :, hh])
                        step(i)

                    def sample_moments():
                        done(30)
                        step(vec.tensor_tensor(o_s[:, 1, :], o_s[:, 0, :], o_s[:, 0, :], ALU.mult))

                    def sample_variance():
                        vec.wait_ge(mom_ps.sem, mom_ps.at(l, 1))
                        step(vec.tensor_copy(v_s[:, 1, :], X[:, 128:192]))
                        done(32)
                        step(vec.tensor_tensor(v_s[:, 0, 0:32], v_s[:, 1, 0:32], v_s[:, 1, 0:32], ALU.mult))
                        done(33)
                        vec.tensor_scalar(v_s[:, 0, 32:64], X[:, 224:256], EPS, None, ALU.add)
                        step(vec.tensor_tensor(v_s[:, 0, 0:32], X[:, 192:224], v_s[:, 0, 0:32], ALU.subtract))
                        done(34)
                        step(vec.tensor_scalar(v_s[:, 0, 0:32], v_s[:, 0, 0:32], 0.0, GN_EPS, ALU.max, ALU.add))
                        step(vec.tensor_tensor(o_s[:, 0, 0:32], o_s[:, 0, 0:32], v_s[:, 1, 0:32], ALU.subtract))

                    def sample_mixed():
                        done(36)
                        vec.wait_ge(s_p.sem, s_p.at(l, 1))
                        step(vec.tensor_tensor(o_s[:, 0, :], o_s[:, 0, :], rs_s[:, :], ALU.mult))
                        done(37)
                        for h in range(HEADS):
                            c = slice(8 * h, 8 * h + 8)
                            vec.tensor_scalar(o_s[:, 0, c], o_s[:, 0, c], parh[:, 1 + h:2 + h], parh[:, 5 + h:6 + h], ALU.mult, ALU.add)
                        step(vec.tensor_scalar(o_s[:, 0, 32:64], o_s[:, 0, 32:64], parh[:, 0:1], None, ALU.mult))
                        vec.wait_ge(tg_s.sem, tg_s.at(l, 2))
                        for g in range(2):
                            sv = sg_s[:, 32 * g:32 * g + 32].rearrange("p (a b) -> p a b", b=8)
                            i = vec.scalar_tensor_tensor(sv, sv, 1.0, z_t[:, 4 + 8 * g:8 + 8 * g, :], ALU.add, ALU.mult)
                        step(i)
                        done(39)
                        step(vec.tensor_tensor(o_s[:, 0, :], o_s[:, 0, :], sg_s[:, :], ALU.mult))
                        done(40)
                        o3 = o_s[:, 0, :].rearrange("p (c b) -> p c b", b=8)
                        vec.tensor_copy(ms[:, 4:8, 0:8], o3[:, 0:4, :])
                        step(vec.tensor_copy(ms[:, 0:4, 0:8], o3[:, 4:8, :]))
                        done(41)
                        vec.tensor_tensor(ms[:, 4:8, 8:16], o3[:, 0:4, :], ms[:, 4:8, 0:8].bitcast(f32), ALU.subtract)
                        step(vec.tensor_tensor(ms[:, 0:4, 8:16], o3[:, 4:8, :], ms[:, 0:4, 0:8].bitcast(f32), ALU.subtract))

                    def sample_residual(u):
                        vec.wait_ge(slot_used, n * SLOTS + (4 * (6 + u) + 5 + RING))
                        c = slice(512 * u, 512 * u + 512)
                        step(vec.tensor_tensor(xs[:, c], OB[0:8, :], xs[:, c], ALU.add))

                    def sample_work(w):
                        if kind == 0:
                            if w == 4:
                                sample_gate()
                            if w == 8:
                                sample_q_ret()
                            if w == 19:
                                sample_q_gla()
                        if kind == 1:
                            if w == 1:
                                sample_decay(0)
                            if w == 12:
                                sample_decay(1)
                            if w - 1 in V_AT:
                                sample_update(V_AT.index(w - 1))
                            if w == 10:
                                sample_o(0)
                            if w == 22:
                                sample_o(1)
                                sample_moments()
                            if w == 23:
                                sample_variance()
                            if w == 24:
                                sample_mixed()
                            if w == 29:
                                sample_residual(0)

                    def keys(g):
                        for hf, src in ((0, X), (1, ATT)):
                            vec.wait_ge(kn_ps.sem, kn_ps.at(n, 2 * g + hf + 1))
                            dst = k_n[:, 2 * hf:2 * hf + 2, :]
                            if g == 0:
                                vec.tensor_tensor(dst.rearrange("p t (h n) -> p t h n", h=HEADS), src[:, :].rearrange("p (t h n) -> p t h n", t=2, h=HEADS),
                                                  kdec[:, :].unsqueeze(1).unsqueeze(3).to_broadcast([128, 2, HEADS, DK]), ALU.mult).then_inc(kn_sb.sem, 1)
                            else:
                                vec.tensor_copy(dst, src[:, :].rearrange("p (t n) -> p t n", t=2)).then_inc(kn_sb.sem, 1)

                    def scores(g, t):
                        vec.wait_ge(att_ps.sem, att_ps.at(n, 4 * g + t + 1))
                        a3 = ATT[:, :].rearrange("p (h n) -> p h n", h=HEADS)
                        if g == 0:
                            vec.tensor_tensor(a_ret[:, :, :], a3, rmask[:, :].rearrange("p (h n) -> p h n", h=HEADS), ALU.mult).then_inc(att_sb.sem, 1)
                        else:
                            apart()
                            vec.copy_predicated(a_gla[:, :, :], gmask[:, :].unsqueeze(1).to_broadcast([128, HEADS, TOK]), a3).then_inc(att_sb.sem, 1)

                    def state(g, t):
                        vec.wait_ge(st_ps.sem, st_ps.at(n, 4 * g + t + 1))
                        if g == 0:
                            if t > 0:
                                vec.wait_ge(sret_sb.sem, sret_sb.at(n, t))
                            for p in range(2):
                                c = slice(256 * p, 256 * p + 256)
                                i = vec.scalar_tensor_tensor(s_ret[:, c], s_ret[:, c], small[:, 6 + p:7 + p], ST[:, c], ALU.mult, ALU.add)
                            i.then_inc(sret_sb.sem, 1)
                            return
                        vec.wait_ge(sgla_sb.sem, sgla_sb.at(n, 1 + 2 * t))
                        vec.tensor_tensor(s_gla[:, :], ST[:, :], s_mid[:, :], ALU.add).then_inc(sgla_sb.sem, 1)
                        vec.wait_ge(sgla_sb.sem, sgla_sb.at(n, 2 + 2 * t))
                        for p in range(2):
                            c = slice(256 * p, 256 * p + 256)
                            if t < TPB - 1:
                                i = vec.tensor_scalar(s_mid[:, c], s_gla[:, c], cc[:, p, t:t + 1], None, ALU.mult)
                            else:
                                i = vec.tensor_scalar(s_gla[:, c], s_gla[:, c], ex[:, p, 0, BLK - 1:BLK], None, ALU.mult)
                        i.then_inc(sgla_sb.sem, 1)

                    def stats(g, t):
                        z, base = t % 2, 3 * t if g == 0 else 12 + 4 * t
                        vec.wait_ge(o_sb.sem, o_sb.at(n, 4 * g + t + 1))
                        for h in range(HEADS):
                            i = vec.bn_stats(bns[:, z, h, :], o_n[:, t, 128 * h:128 * h + 128])
                        i.then_inc(ostat.sem, 1)
                        vec.wait_ge(ostat.sem, ostat.at(n, base + 1))
                        apart()
                        for h in range(HEADS):
                            i = vec.bn_aggr(agg[:, z, h, :], bns[:, z, h, :])
                        i.then_inc(ostat.sem, 1)
                        vec.wait_ge(ostat.sem, ostat.at(n, base + 2))
                        if g == 0:
                            vec.tensor_scalar(var[:, z, :], agg[:, z, :, 1], GN_EPS, None, ALU.add).then_inc(ostat.sem, 1)
                        else:
                            vec.tensor_tensor(msq[:, z, :], agg[:, z, :, 0], agg[:, z, :, 0], ALU.mult).then_inc(ostat.sem, 1)
                            vec.wait_ge(ostat.sem, ostat.at(n, base + 3))
                            vec.scalar_tensor_tensor(var[:, z, :], msq[:, z, :], EPS, agg[:, z, :, 1], ALU.add, ALU.add).then_inc(ostat.sem, 1)

                    def norm(g, t):
                        z = t % 2
                        vec.wait_ge(rstd_o.sem, rstd_o.at(n, 4 * g + t + 1))
                        for h in range(HEADS):
                            oh = o_n[:, t, 128 * h:128 * h + 128]
                            if g == 0:
                                i = vec.tensor_scalar(oh, oh, agg[:, z, h, 0:1], rstd[:, z, h:h + 1], ALU.subtract, ALU.mult)
                            else:
                                i = vec.tensor_scalar(oh, oh, rstd[:, z, h:h + 1], None, ALU.mult)
                        i.then_inc(normed.sem, 1)

                    def silu(g):
                        for q in range(4):
                            vec.wait_ge(g_tanh.sem, g_tanh.at(n, 4 * g + q + 1))
                            vec.scalar_tensor_tensor(g_t[:, q, :], g_t[:, q, :], 1.0, P[q][:, :], ALU.add, ALU.mult).then_inc(g_silu.sem, 1)

                    def mixed(g, t):
                        gate = g_t[:, :, TOK * t:TOK * t + TOK]
                        dst = tmp[:, t % 2, :].rearrange("p (h n) -> p h n", h=HEADS)
                        if g == 0:
                            vec.wait_ge(m_aff.sem, m_aff.at(n, t + 1))
                            if t == 0:
                                vec.wait_ge(g_silu.sem, g_silu.at(n, 4))
                            vec.tensor_tensor(dst, dst, gate, ALU.mult).then_inc(mix_sb.sem, 1)
                        else:
                            vec.wait_ge(mt_ps.sem, mt_ps.at(n, 4 + t + 1))
                            if t == 0:
                                vec.wait_ge(g_silu.sem, g_silu.at(n, 8))
                            vec.wait_ge(mlo_sb.sem, mlo_sb.at(n, 4 + t - 1 if t >= 2 else 4))
                            src = (X if t % 2 == 0 else ST)[:, :].rearrange("p (h n) -> p h n", h=HEADS)
                            vec.scalar_tensor_tensor(dst, src, parh[:, 0:1], gate, ALU.mult, ALU.mult).then_inc(mix_sb.sem, 1)

                    def rotate():
                        for p in range(2):
                            wait_bank(vec, n, 0, p)
                            if p == 0:
                                vec.wait_ge(stored.sem, stored.at(n, 0))
                            q4 = [a.rearrange("p (t n) -> p t n", t=TPB) for a in (q_t[:, p, 0, :], P[p][:, :])]
                            vec.tensor_tensor(q4[0], q4[1], qdec[:, p, :].unsqueeze(1).to_broadcast([128, TPB, TOK]), ALU.mult).then_inc(q_raw.sem, 1)
                        vec.wait_ge(rope_in.sem, rope_in.at(n, 16))
                        vec.wait_ge(la_sb.sem, la_sb.at(n, 2))
                        c = 0
                        for i_ in (2, 3, 0, 1):
                            buf = q_t[:, i_, 0, :] if i_ < 2 else k_t[:, i_ - 2, :]
                            if i_ < 2:
                                vec.wait_ge(q_raw.sem, q_raw.at(n, i_ + 1))
                            else:
                                vec.wait_ge(k_raw.sem, k_raw.at(n, i_ - 1))
                            if c > 0:
                                vec.wait_ge(rope_st.sem, rope_st.at(n, c))
                            apart()
                            vec.stream_shuffle(r_tmp[:, :], buf, [(p + 16) % 32 for p in range(32)]).then_inc(rope_st.sem, 1)
                            vec.wait_ge(rope_st.sem, rope_st.at(n, c + 1))
                            vec.tensor_tensor(buf, buf, rope[:, 0, :], ALU.mult).then_inc(rope_st.sem, 1)
                            vec.wait_ge(rope_st.sem, rope_st.at(n, c + 2))
                            vec.tensor_tensor(r_tmp[:, :], r_tmp[:, :], rope[:, 1, :], ALU.mult).then_inc(rope_st.sem, 1)
                            vec.wait_ge(rope_st.sem, rope_st.at(n, c + 3))
                            if i_ < 2:
                                vec.memset(q_t[0:64, i_, 1, :], 0.0)
                                vec.tensor_tensor(q_t[64:128, i_, 1, :], buf[64:128, :], r_tmp[64:128, :], ALU.add)
                                vec.tensor_tensor(buf[0:64, :], buf[0:64, :], r_tmp[0:64, :], ALU.add).then_inc(rope_st.sem, 1)
                                vec.wait_ge(rope_st.sem, rope_st.at(n, c + 4))
                                vec.memset(buf[64:128, :], 0.0).then_inc(rope_st.sem, 1)
                                c += 5
                            else:
                                vec.tensor_tensor(buf, buf, r_tmp[:, :], ALU.add).then_inc(rope_st.sem, 1)
                                c += 4

                    if kind == 0:
                        sample_start()
                    for w in range(1, SLOTS):
                        if w in (3, 4):
                            hf = w - 3
                            vec.wait_ge(gate_l.sem, gate_l.at(n, 3 * hf + 3))
                            vec.scalar_tensor_tensor(la[:, 2 * hf:2 * hf + 2, :].rearrange("p a n -> p (a n)"), (ATT, OB)[hf][:, :], 0.0, tmp[:, hf, :],
                                                     ALU.min, ALU.subtract).then_inc(la_sb.sem, 1)
                        if w == 5:
                            rotate()
                        if w == 8:
                            vec.wait_ge(ex_sb.sem, ex_sb.at(n, 4))
                            vec.wait_ge(em_sb.sem, em_sb.at(n, 1))
                            for p in range(2):
                                i = vec.tensor_tensor(cc[:, p, 0:TPB - 1], ex[:, p, 0, TOK - 1:BLK - TOK:TOK], em[:, 1:TPB, p, 0], ALU.mult)
                            i.then_inc(cc_sb.sem, 1)
                            for p in range(2):
                                c = slice(256 * p, 256 * p + 256)
                                i = vec.tensor_scalar(s_mid[:, c], s_gla[:, c], em[:, 0, p, 0:1], None, ALU.mult)
                            i.then_inc(sgla_sb.sem, 1)
                        if w == 13:
                            silu(0)
                        if w == 17:
                            for p in range(2):
                                wait_bank(vec, n, 3, p)
                                for hh in range(2):
                                    r = slice(64 * hh, 64 * hh + 64)
                                    i = vec.scalar_tensor_tensor(q_t[r, p, hh, :], P[p][r, :], DK ** -0.5, ex[r, p, 0, :], ALU.mult, ALU.mult)
                                i.then_inc(qk_gla.sem, 1)
                            for p in range(2):
                                wait_bank(vec, n, 3, 2 + p)
                                vec.tensor_tensor(k_t[:, p, :], P[2 + p][:, :], ex[:, p, 1, :], ALU.mult).then_inc(qk_gla.sem, 1)
                        if w == 25:
                            silu(1)
                        if w in (8, 20):
                            keys(w // 20)
                        for g, first in ((0, 9), (1, 21)):
                            t = w - first
                            if 0 <= t < TPB:
                                scores(g, t)
                            if 1 <= t <= TPB:
                                state(g, t - 1)
                            if 2 <= t <= TPB + 1:
                                norm(g, t - 2)
                            if 1 <= t <= TPB:
                                stats(g, t - 1)
                        if 14 <= w < 18:
                            mixed(0, w - 14)
                        if w == 18:
                            next_norm(vec, n + 1)
                        if w in (26, 27):
                            mixed(1, 2 * (w - 26))
                            mixed(1, 2 * (w - 26) + 1)
                        if w == 29:
                            vec.wait_ge(res_in.sem, res_in.at(n, 16))
                            for q in range(4):
                                wait_bank(vec, n, 6, q)
                                vec.tensor_tensor(y_t[:, q, 0:512], P[q][:, :], y_t[:, q, 0:512], ALU.add).then_inc(y_add.sem, 1)
                        if w == 28:
                            vec.memset(lr_t, 1.0).then_inc(lr_ones.sem, 1)
                        if 28 <= w < 32:
                            next_lo(vec, n + 1, 2 * (w - 28))
                            next_lo(vec, n + 1, 2 * (w - 28) + 1)
                        sample_work(w)
                    for q in range(4):
                        wait_bank(vec, n, 7, q)
                        vec.tensor_tensor(y_t[:, q, 512:1024], P[q][:, :], y_t[:, q, 512:1024], ALU.add).then_inc(y_add.sem, 1)
                    vec.wait_ge(y_add.sem, y_add.at(n, 8))
                    stats_steps(vec, y_t, ystat, n, "y")
                    vec.wait_ge(rstd_y.sem, rstd_y.at(n, 1))
                    vec.wait_ge(fin_in.sem, fin_in.at(n, 16))
                    for t in range(TPB):
                        i = vec.scalar_tensor_tensor(yn[:, t, :], y_t[:, t, :], yrs[:, t:t + 1], fin_w[:, :], ALU.mult, ALU.mult)
                    i.then_inc(yn_sb.sem, 1)
                    if kind == 1:
                        sample_residual(1)
                        done(44)
                        sample_norm(l, 44)

                blocks(vec, l, body)


def rotary_tables():
    row = np.arange(128) % 64
    quarter, second, i = row // 32, (row % 32) // 16, row % 16
    halfdim = DK // 2
    inv = (ROPE_BASE ** (-np.arange(halfdim) / halfdim)).astype(np.float32)
    freq = inv[quarter * 16 + i]
    sign = np.where(second == 1, 1.0, -1.0)
    gamma = 1.0 - 2.0 ** (-5.0 - np.arange(HEADS))

    def tables(pos):
        ang = (pos.astype(np.float32)[None, :] * freq[:, None]).astype(np.float32).astype(np.float64)
        return np.cos(ang), np.sin(ang) * sign[:, None]

    cos, sin = tables(np.arange(SEQ))
    head = np.arange(128) // 64
    out = np.stack([tab.reshape(128, NBLK, BLK).transpose(1, 0, 2) for tab in (cos, sin)], axis=2).astype(np.float32)
    qdec = np.stack([gamma[2 * p + head][:, None] ** (np.arange(TOK) + 1.0)[None, :] for p in range(2)], axis=1).astype(np.float32)
    small = np.zeros((128, 16), np.float32)
    cs, sn = tables(np.array([PAST]))
    small[:, 0], small[:, 1] = cs[:, 0], sn[:, 0]
    small[:, 2], small[:, 3] = cs[:, 0] * DK ** -0.5, sn[:, 0] * DK ** -0.5
    for p in range(2):
        small[:, 4 + p] = gamma[2 * p + head]
        small[:, 6 + p] = gamma[2 * p + head] ** TOK
    return out, qdec, small, gamma


def kernel(x_prompt, x_sample, state_gla, state_ret, norm_w, w_in, gla_w2, gla_b,
           gla_norm_w, ret_norm_w, ret_norm_b, w_out, final_norm_w):
    import concourse.bacc as bacc
    from concourse.bass_utils import run_bass_kernel_spmd

    f = {k: np.asarray(v) for k, v in dict(x_prompt=x_prompt, x_sample=x_sample, state_gla=state_gla, state_ret=state_ret,
         norm_w=norm_w, w_in=w_in, gla_w2=gla_w2, gla_b=gla_b, gla_norm_w=gla_norm_w, ret_norm_w=ret_norm_w,
         ret_norm_b=ret_norm_b, w_out=w_out, final_norm_w=final_norm_w).items()}
    perm = np.arange(64).reshape(2, 2, 16).transpose(1, 0, 2).reshape(64)
    heads_perm = np.concatenate([64 * h + perm for h in range(8)])
    cols = np.cumsum([0, 256, 256, 512, 512, 16, 256, 256, 512, 512])
    w_in, w_out = f["w_in"], f["w_out"]
    slots = np.empty((DEPTH * SLOTS + 3, 128, 1024), np.float32)
    units = [w_in[:, :, cols[5]:cols[7]][:, :, heads_perm], w_in[:, :, cols[7]:cols[8]], w_in[:, :, cols[8]:cols[9]],
             w_in[:, :, 0:512], w_in[:, :, 512:1024], w_in[:, :, 1024:1536],
             np.roll(w_out[:, :, 0:512], -512, axis=1), np.roll(w_out[:, :, 512:1024], -512, axis=1)]
    for l in range(DEPTH):
        gate = w_in[l][:, cols[4]:cols[4] + 128]
        slots[l * SLOTS] = gate.reshape(KT, 128, 128).transpose(1, 0, 2).reshape(128, 1024)
        for u, w in enumerate(units):
            for s in range(4):
                slots[l * SLOTS + 1 + 4 * u + s] = w[l][256 * s:256 * s + 256].reshape(2, 128, 512).transpose(1, 0, 2).reshape(128, 1024)
    slots[DEPTH * SLOTS:] = slots[0:3]
    par = np.empty((DEPTH, 128, 17), np.float32)
    for l in range(DEPTH):
        par[l, :, 0:8] = f["norm_w"][l].reshape(KT, 128).T
        par[l, :, 8] = f["gla_norm_w"][l]
        par[l, :, 9:13] = f["ret_norm_w"][l].reshape(HEADS, DV).T
        par[l, :, 13:17] = f["ret_norm_b"][l].reshape(HEADS, DV).T
    nw_all = np.stack([par[min(m // NBLK, DEPTH - 1), :, 0:8] for m in range(DEPTH * NBLK + 1)])
    w2b = np.concatenate([f["gla_w2"], f["gla_b"][:, None, :]], axis=1)

    def state_in(s, order):
        s = s[:, :, :, order, :].reshape(DEPTH, DECB, 2, 2, 64, DV)
        return np.ascontiguousarray(s.transpose(0, 2, 3, 4, 1, 5).reshape(DEPTH * 2, 128, DECB, DV))

    rope, qdec, small, gamma = rotary_tables()
    s_, t_ = np.arange(TOK)[:, None], np.arange(TOK)[None, :]
    cum = np.zeros((128, 130), np.float32)
    cum[:, 0:128] = ((s_ <= t_).astype(np.float32) - (s_ <= MID)) / TAU
    cum[:, 128:130] = (s_ <= MID) / TAU
    rmask = np.stack([(s_ <= t_) * gamma[h] ** -(s_ + 1.0) * DK ** -0.5 for h in range(HEADS)], axis=1).reshape(128, 512).astype(np.float32)
    kdec = (gamma[None, :] ** (TOK - 1.0 - np.arange(TOK))[:, None] * DK ** -0.5).astype(np.float32)
    comb = np.zeros((16, 8), np.float32)
    for b in range(DECB):
        comb[b, b] = comb[8 + b, b] = 1.0
    ins = dict(
        x_prompt=f["x_prompt"].reshape(SEQ, D), x_sample=f["x_sample"].reshape(DECB, D),
        state_gla=state_in(f["state_gla"], np.arange(64)), state_ret=state_in(f["state_ret"], perm),
        w_slots=slots, par=par, nw_all=nw_all, w2b=w2b, rope=rope, small=small, cum=cum, rmask=rmask, kdec=kdec, qdec=qdec,
        ident=np.eye(128, dtype=np.float32), comb=comb,
        ones=np.full((128, 128), 1.0 / DV, np.float32),
        fin_w=np.broadcast_to(f["final_norm_w"][None, :], (128, D)))
    outs = dict(y_prompt=(SEQ, D), y_sample=(DECB, D), gla_p=(DEPTH, 128, 512), ret_p=(DEPTH, 128, 512),
                gla_s=(DEPTH * 2, 128, DECB, DV), ret_s=(DEPTH * 2, 128, DECB, DV), acts=(SEQ, D))
    nc = bacc.Bacc("TRN2", target_bir_lowering=False, num_devices=1)
    arrays, d = {}, {}
    for name, a in ins.items():
        arrays["in_" + name] = np.ascontiguousarray(a)
        d[name] = nc.dram_tensor("in_" + name, a.shape, mybir.dt.from_np(a.dtype), kind="ExternalInput").ap()
    for name, shape in outs.items():
        kind = "Internal" if name == "acts" else "ExternalOutput"
        d[name] = nc.dram_tensor("out_" + name, shape, mybir.dt.float32, kind=kind).ap()
    build(nc, d)
    r = run_bass_kernel_spmd(nc, [arrays], core_ids=[0]).results[0]
    inv = np.argsort(perm)

    def prompt_state(a, order):
        a = a.reshape(DEPTH, 2, 64, 2, 2, DV)
        a = np.stack([a[:, h % 2, :, h // 2, h % 2, :] for h in range(HEADS)], axis=1)
        return a[:, None, :, order, :]

    def sample_state(a, order):
        a = a.reshape(DEPTH, 2, 2, 64, DECB, DV).transpose(0, 4, 1, 2, 3, 5).reshape(DEPTH, DECB, HEADS, 64, DV)
        return a[:, :, :, order, :]

    same = np.arange(64)
    return (r["out_y_prompt"].reshape(1, SEQ, D), r["out_y_sample"].reshape(DECB, 1, D),
            prompt_state(r["out_gla_p"], same), prompt_state(r["out_ret_p"], inv),
            sample_state(r["out_gla_s"], same), sample_state(r["out_ret_s"], inv))
```

```python
import itertools
from contextlib import ExitStack

import numpy as np

import concourse.bass as bass
from concourse import mybir

D, SEQ, DEPTH, DECB, PAST = 1024, 2048, 2, 8, 16384
HEADS, DK, DV, RANK = 4, 64, 128, 16
EPS, GN_EPS, TAU, ROPE_BASE = 1e-6, 1e-5, 16.0, 10000.0
TOK = 128
BLK = 512
TPB = BLK // TOK
NBLK = SEQ // BLK
KT = D // 128
GATE = KT * RANK
SLOTS = 33
RING = 3
AHEAD = 2
Z_BANK = "SSXSSX"
Z_READ = (5, 9, 13, 17, 21, 25)
V_AT = (0, 1, 2, 3, 4, 6, 7, 8) + tuple(range(11, 19))
V_H, V_LA = 3, 4
V_DEC = (11, 21)
V_O = (20, 30)
V_SQ, V_MOM, V_VAR, V_MIX = 31, 34, 35, 42
V_X0, V_X1, V_NV, V_LAST = 44, 46, 50, 52
MID = TOK // 2 - 1


class Count:

    def __init__(self, sem, per, base=0):
        self.sem, self.per, self.base = sem, per, base

    def at(self, n, k):
        return n * self.per + (self.base + k)


def build(nc, d):
    f32, f32r, u8 = mybir.dt.float32, mybir.dt.float32r, mybir.dt.uint8
    ALU, ACT = mybir.AluOpType, mybir.ActivationFunctionType
    ctx = ExitStack()
    with ctx:
        def sb(name, shape, dt=f32):
            return ctx.enter_context(nc.sbuf_tensor(name, shape, dt))

        def sem(name):
            return ctx.enter_context(nc.semaphore(name))

        w_stage = sb("w_stage", [128, RING, 512])
        w_lo = sb("w_lo", [128, RING, 1024], f32r)
        w_hi = sb("w_hi", [128, RING, 1024], f32r)
        xn = sb("xn", [128, TPB, D])
        h_hi = sb("h_hi", [128, KT, BLK], f32r)
        h_lo = sb("h_lo", [128, KT, BLK], f32r)
        m_hi = sb("m_hi", [128, KT, BLK], f32r)
        m_lo = sb("m_lo", [128, KT, BLK], f32r)
        region = sb("region", [128, 9216])
        q_t = region[:, 0:2048].rearrange("p (i h n) -> p i h n", i=2, h=2)
        v_n = region[:, 2048:4096].rearrange("p (t n) -> p t n", t=TPB)
        y_t = region[:, 0:4096].rearrange("p (t n) -> p t n", t=TPB)
        g_t = region[:, 4096:6144].rearrange("p (h n) -> p h n", h=HEADS)
        o_n = region[:, 6144:8192].rearrange("p (t n) -> p t n", t=TPB)
        yn = region[:, 4096:8192].rearrange("p (t n) -> p t n", t=TPB)
        k_t = region[:, 8192:9216].rearrange("p (i n) -> p i n", i=2)
        rope = sb("rope", [128, 2, BLK])
        ex = sb("ex", [128, 2, 2, BLK])
        fin_w = ex[:, 0, :, :].rearrange("p a n -> p (a n)")
        em = sb("em", [128, TPB, 2, 2])
        cc = sb("cc", [128, 2, TPB])
        spare = sb("spare", [128, 32])
        la = sb("la", [128, TPB, 256])
        tmp = sb("tmp", [128, 2, BLK])
        r_tmp = tmp[:, 0, :]
        lr_t = k_t[0:64, 0, :]
        k_n = sb("k_n", [128, TPB, 256])
        a_ret = tmp[:, 1, :].rearrange("p (h n) -> p h n", h=HEADS)
        a_gla = sb("a_gla", [128, HEADS, TOK])
        s_ret = sb("s_ret", [128, 512])
        s_gla = sb("s_gla", [128, 512])
        s_mid = sb("s_mid", [128, 512])
        bns = sb("bns", [128, 2, HEADS, 6])
        agg = sb("agg", [128, 2, HEADS, 2])
        msq = sb("msq", [128, 2, HEADS])
        var = sb("var", [128, 2, HEADS])
        rstd = sb("rstd", [128, 2, HEADS])
        xbn = sb("xbn", [128, TPB, 12])
        xagg = sb("xagg", [128, TPB, 2])
        xms = sb("xms", [128, TPB])
        xvar = sb("xvar", [128, TPB])
        xrs = sb("xrs", [128, TPB])
        yrs = sb("yrs", [128, TPB])
        ident = sb("ident", [128, 128])
        cum = sb("cum", [128, 130])
        gmask = sb("gmask", [128, TOK], u8)
        rmask = sb("rmask", [128, HEADS * TOK])
        kdec = sb("kdec", [128, HEADS])
        qdec = sb("qdec", [128, 2, TOK])
        small = sb("small", [128, 16])
        half = sb("half", [128, 24])
        nw = sb("nw", [128, KT])
        par = sb("par", [128, 17])
        parh = sb("parh", [128, 9])
        w2b = sb("w2b", [2 * RANK + 1, 256])
        comb = sb("comb", [16, 64])
        ones = sb("ones", [128, 128])
        ss = sb("ss", [128, 2, DECB, DV])
        ys = ss[0:8, 0, :, :].rearrange("p b n -> p (b n)")
        v_b = sb("v_b", [128, 512])
        z = sb("z", [16, 2, 512])
        z_u, z_v = z[:, 0, :], z[:, 1, :]
        xs = sb("xs", [8, D])
        xsn = z[0:8, :, :].rearrange("p a n -> p (a n)")
        hs = sb("hs", [128, KT, 16], f32r)
        ms = sb("ms", [128, KT, 40], f32r)
        lr_s = sb("lr_s", [64, 8])
        z_t = sb("z_t", [128, 16, 8])
        rot = sb("rot", [128, 4, 8])
        gt, al = sb("gt", [128, 16]), sb("al", [128, 16])
        q_s = sb("q_s", [128, 2, 2, 8, 2])
        k_s = sb("k_s", [128, 2, 2, 8])
        o_s = sb("o_s", [128, 2, 64])
        hs_f = o_s[:, 0, :]
        v_s = sb("v_s", [128, 2, 64])
        sg_s, rs_s = sb("sg_s", [128, 64]), sb("rs_s", [128, 64])
        sbn, sagg = sb("sbn", [8, 12]), sb("sagg", [8, 2])
        smsq, svar, srs = sb("smsq", [8, 1]), sb("svar", [8, 1]), sb("srs", [8, 1])

        bank = [ctx.enter_context(nc.psum_tensor(f"bank{i}", [128, 512], f32)) for i in range(8)]
        P, ATT, OB, ST, X = bank[0:4], bank[4], bank[5], bank[6], bank[7]

        w_loaded = [sem(f"w_loaded{r}") for r in range(RING)]
        hi_done, lo_done, slot_used = sem("hi_done"), sem("lo_done"), sem("slot_used")
        const_in, par_in, sets = sem("const_in"), sem("par_in"), sem("sets")
        x_in, nw_in, rope_in, res_in, fin_in = (
            Count(sem(n), k, base) for n, k, base in (("x_in", 64, -64), ("nw_in", 16, 0), ("rope_in", 16, 0), ("res_in", 64, 0), ("fin_in", 16, 0)))
        x_first = [sem(f"x_first{t}") for t in range(TPB)]
        stored = Count(sem("stored"), 64, base=16)
        state_in, state_out, st_saved = sem("state_in"), sem("state_out"), sem("st_saved")
        proj = Count(sem("proj"), 24)
        gate_x, cum_b, mid_b = Count(sem("gate_x"), 2), Count(sem("cum_b"), 2), Count(sem("mid_b"), 1)
        kn_ps, kn_sb = Count(sem("kn_ps"), 4), Count(sem("kn_sb"), 4)
        att_ps, o_ps, st_ps, mt_ps = (Count(sem(n), 8) for n in ("att_ps", "o_ps", "st_ps", "mt_ps"))
        ht_ps = Count(sem("ht_ps"), 8)
        lr_sb, gate_l, ex_sb, em_sb = Count(sem("lr_sb"), 1), Count(sem("gate_l"), 6), Count(sem("ex_sb"), 4), Count(sem("em_sb"), 1)
        k_raw, v_sb, g_tanh, o_sb = Count(sem("k_raw"), 2), Count(sem("v_sb"), 8), Count(sem("g_tanh"), 8), Count(sem("o_sb"), 8)
        m_aff, mhi_sb, hhi_sb = Count(sem("m_aff"), 4), Count(sem("mhi_sb"), 8), Count(sem("hhi_sb"), 8)
        lr_ones = Count(sem("lr_ones"), 1)
        la_sb, q_raw, rope_st, qk_gla = Count(sem("la_sb"), 2), Count(sem("q_raw"), 2), Count(sem("rope_st"), 18), Count(sem("qk_gla"), 4)
        att_sb, sret_sb = Count(sem("att_sb"), 8), Count(sem("sret_sb"), 4)
        sgla_sb, cc_sb = Count(sem("sgla_sb"), 9), Count(sem("cc_sb"), 1)
        ostat, normed, g_silu = Count(sem("ostat"), 28), Count(sem("normed"), 8), Count(sem("g_silu"), 8)
        mix_sb, y_add, hlo_sb = Count(sem("mix_sb"), 8), Count(sem("y_add"), 8, base=8), Count(sem("hlo_sb"), 8)
        xstat, xn_sb, ystat, yn_sb = Count(sem("xstat"), 4), Count(sem("xn_sb"), 1), Count(sem("ystat"), 4), Count(sem("yn_sb"), 4)
        rstd_o, rstd_x, rstd_y, mlo_sb = Count(sem("rstd_o"), 8), Count(sem("rstd_x"), 1), Count(sem("rstd_y"), 1), Count(sem("mlo_sb"), 8)
        s_v = Count(sem("s_v"), V_LAST, base=6)
        s_p = Count(sem("s_p"), 4, base=1)
        v_out, v_in = sem("v_out"), Count(sem("v_in"), 16 * 2 * DECB)
        xs_t, zt_ps, gx_ps, vn_ps, vn_sb = (Count(sem(n), k) for n, k in (("xs_t", 1), ("zt_ps", 5), ("gx_ps", 1), ("vn_ps", 2), ("vn_sb", 2)))
        so_ps, mom_ps = Count(sem("so_ps"), 2), Count(sem("mom_ps"), 1)
        z_sb, zt_sb, gl_s, al_s, tg_s = (Count(sem(n), k) for n, k in (("z_sb", 7), ("zt_sb", 5), ("gl_s", 3), ("al_s", 1), ("tg_s", 2)))
        fin_out = sem("fin_out")

        columns = itertools.cycle(range(30))

        def apart():
            c = next(columns)
            nc.vector.memset(spare[:, c:c + 1], 0.0)

        w_gate = w_hi[:, 0, 0:2 * GATE].rearrange("p (k n) -> p k n", k=KT)

        def gate(h):
            return h // 2 % SLOTS == 0

        def load_half(act, first_row, n, h):
            act.wait_ge(lo_done, n * 2 * SLOTS + (h + 1))
            cols = GATE // 2 if gate(h) else 512
            act.dma_start(w_stage[:, h % RING, 0:cols], d["w_slots"][bass.ds(first_row + h // 2, 1), :, 512 * (h % 2):512 * (h % 2) + cols].rearrange("s p n -> (s p) n")
                          ).then_inc(w_loaded[h % RING], 16)

        def split_hi(act, n, h):
            act.wait_ge(w_loaded[h % RING], n * (2 * SLOTS // RING * 16) + (h // RING + 1) * 16)
            if h % 2 == 0:
                act.wait_ge(slot_used, n * SLOTS + (h // 2 + 1))
            if gate(h):
                src = w_stage[:, h % RING, 0:GATE // 2].rearrange("p (k n) -> p k n", n=RANK)
                nc.scalar.activation(w_gate[:, h % 2 * 4:h % 2 * 4 + 4, 0:RANK], src, ACT.Copy).then_inc(hi_done, 1)
            else:
                c = slice(512 * (h % 2), 512 * (h % 2) + 512)
                nc.scalar.activation(w_hi[:, h // 2 % RING, c], w_stage[:, h % RING, :], ACT.Copy).then_inc(hi_done, 1)

        def split_lo(pool, n, h):
            pool.wait_ge(hi_done, n * 2 * SLOTS + (h + 1))
            if gate(h):
                src = w_stage[:, h % RING, 0:GATE // 2].rearrange("p (k n) -> p k n", n=RANK)
                k = slice(h % 2 * 4, h % 2 * 4 + 4)
                pool.tensor_tensor(w_gate[:, k, RANK:2 * RANK], src, w_gate[:, k, 0:RANK].bitcast(f32), ALU.subtract).then_inc(lo_done, 1)
            else:
                r, c = h // 2 % RING, slice(512 * (h % 2), 512 * (h % 2) + 512)
                pool.tensor_tensor(w_lo[:, r, c], w_stage[:, h % RING, :], w_hi[:, r, c].bitcast(f32), ALU.subtract).then_inc(lo_done, 1)

        def wait_slot(pe, n, j):
            pe.wait_ge(lo_done, n * 2 * SLOTS + (2 * j + 2 + RING))

        def blocks(eng, l, body):
            for kind in range(2):
                with eng.Fori(kind, kind + 1) as b:
                    body(l * NBLK + b, l * SLOTS, kind)
            with eng.Fori(2, NBLK) as b:
                body(l * NBLK + b, (l + b - 2) * SLOTS, 2)

        def wait_bank(eng, n, u, j):
            if j < 3:
                eng.wait_ge(proj.sem, proj.at(n, 3 * u + j + 1))
            else:
                eng.wait_ge(slot_used, n * SLOTS + (4 * u + 5 + RING))

        def tile_stats(vec, buf, t, halves=(0, 1)):
            for s in halves:
                i = vec.bn_stats(xbn[:, t, 6 * s:6 * s + 6], buf[:, t, 512 * s:512 * s + 512])
            return i

        def mean_square(vec, count, n):
            vec.wait_ge(count.sem, count.at(n, 1))
            apart()
            for t in range(TPB):
                i = vec.bn_aggr(xagg[:, t, :], xbn[:, t, :])
            i.then_inc(count.sem, 1)
            vec.wait_ge(count.sem, count.at(n, 2))
            vec.tensor_tensor(xms[:, :], xagg[:, :, 0], xagg[:, :, 0], ALU.mult).then_inc(count.sem, 1)
            vec.wait_ge(count.sem, count.at(n, 3))
            vec.scalar_tensor_tensor(xvar[:, :], xms[:, :], EPS, xagg[:, :, 1], ALU.add, ALU.add).then_inc(count.sem, 1)

        def next_stats(vec, m, first=False):
            if not first:
                vec.wait_ge(x_in.sem, x_in.at(m, 64))
            for t in range(TPB):
                if first:
                    vec.wait_ge(x_first[t], 16)
                i = tile_stats(vec, xn, t)
            i.then_inc(xstat.sem, 1)
            mean_square(vec, xstat, m)

        def next_norm(vec, m):
            vec.wait_ge(rstd_x.sem, rstd_x.at(m, 1))
            for t in range(TPB):
                i = vec.tensor_scalar(xn[:, t, :], xn[:, t, :], xrs[:, t:t + 1], None, ALU.mult)
            i.then_inc(xn_sb.sem, 1)

        def next_hi(act, m, k):
            if k == 0:
                act.wait_ge(nw_in.sem, nw_in.at(m, 16))
            act.wait_ge(ht_ps.sem, ht_ps.at(m, k + 1))
            nc.scalar.activation(h_hi[:, k, :], (X if k % 2 == 0 else ATT)[:, :], ACT.Copy, scale=nw[:, k:k + 1]).then_inc(hhi_sb.sem, 1)

        def next_lo(vec, m, k):
            vec.wait_ge(hhi_sb.sem, hhi_sb.at(m, k + 1))
            vec.scalar_tensor_tensor(h_lo[:, k, :], (X if k % 2 == 0 else ATT)[:, :], nw[:, k:k + 1], h_hi[:, k, :].bitcast(f32),
                                     ALU.mult, ALU.subtract).then_inc(hlo_sb.sem, 1)

        def next_transpose(pe, m, k):
            if k == 0:
                pe.wait_ge(xn_sb.sem, xn_sb.at(m, 1))
            dst = X if k % 2 == 0 else ATT
            if k >= 2:
                pe.wait_ge(hlo_sb.sem, hlo_sb.at(m, k - 1))
            for t in range(TPB):
                i = pe.transpose(dst[:, TOK * t:TOK * t + TOK], xn[:, t, 128 * k:128 * k + 128], ident[:, :])
            i.then_inc(ht_ps.sem, 1)

        block = ctx.enter_context(nc.Block())

        @block.sync
        def _(sp):
            def window(n, w):
                sp.wait_ge(slot_used, n * SLOTS + (w + RING))

            def load_next(m, t):
                src = d["x_prompt"] if m < NBLK or m == DEPTH * NBLK else d["acts"]
                if src is d["acts"]:
                    sp.wait_ge(stored.sem, stored.at(m - NBLK + 1, 0))
                c = m % NBLK * BLK + t * TOK
                sp.dma_start(xn[:, t, :], src[c:c + TOK, :]).then_inc(x_in.sem if m > 0 else x_first[t], 16)

            def load_nw(m):
                sp.dma_start(nw[:, :], d["nw_all"][m, :, :]).then_inc(nw_in.sem, 16)

            def store_out(n, t):
                l, b = n // NBLK, n % NBLK
                rows = slice(b * BLK + t * TOK, b * BLK + t * TOK + TOK)
                if l < DEPTH - 1:
                    sp.wait_ge(y_add.sem, y_add.at(n, 4 + t + 1))
                    if t == TPB - 1:
                        sp.wait_ge(yn_sb.sem, yn_sb.at(n, 4))
                    sp.dma_start(d["acts"][rows, :], y_t[:, t, :]).then_inc(stored.sem, 16)
                else:
                    sp.wait_ge(yn_sb.sem, yn_sb.at(n, t + 1))
                    sp.dma_start(d["y_prompt"][rows, :], yn[:, t, :]).then_inc(stored.sem, 16)

            def load_par(l):
                sp.dma_start(par[:, :], d["par"][l, :, :]).then_inc(par_in, 16)
                sp.dma_start(w2b[:, :], d["w2b"][l, :, :]).then_inc(par_in, 16)

            def load_states(l, name):
                for i in range(2):
                    sp.dma_start(ss[:, i, :, :], d[name][l * 2 + i, :, :, :]).then_inc(state_in, 16)

            def save_states(l, name):
                for i in range(2):
                    sp.dma_start(d[name][l * 2 + i, :, :, :], ss[:, i, :, :]).then_inc(state_out, 16)

            def save_v(l, g):
                sp.wait_ge(vn_sb.sem, vn_sb.at(l, g + 1))
                sp.dma_start(d["v_s"][2 * l + g, :, :], z_v[0:8, :]).then_inc(v_out, 16)

            for t in range(TPB):
                load_next(0, t)
            load_nw(0)
            for dst, name in ((ident, "ident"), (xs, "x_sample"), (cum, "cum"), (rmask, "rmask"), (kdec, "kdec"), (qdec, "qdec"),
                              (small, "small"), (comb, "comb"), (ones, "ones")):
                sp.dma_start(dst[:], d[name]).then_inc(const_in, 16)
            load_par(0)
            for n in range(DEPTH * NBLK):
                l, b = n // NBLK, n % NBLK
                if n > 0:
                    sp.wait_ge(rope_st.sem, rope_st.at(n - 1, 18))
                sp.dma_start(rope[:, :, :], d["rope"][b, :, :, :]).then_inc(rope_in.sem, 16)
                for w in range(20):
                    if w < TPB and n > 0:
                        if w > 0:
                            window(n, w)
                        store_out(n - 1, w)
                    if w == 3:
                        sp.wait_ge(ht_ps.sem, ht_ps.at(n, 8))
                        sp.wait_ge(hlo_sb.sem, hlo_sb.at(n, 8))
                        load_nw(n + 1)
                    if 4 <= w < 8:
                        window(n, w)
                        load_next(n + 1, w - 4)
                    if b == 1:
                        if w in V_AT:
                            c = V_AT.index(w)
                            sp.wait_ge(v_out, 16 * (2 * l + c // DECB + 1))
                            if c > 0:
                                sp.wait_ge(s_v.sem, s_v.at(l, V_DEC[(c - 1) // DECB] + (c - 1) % DECB + 1))
                            sp.dma_start(v_b[:, :], d["v_s"][2 * l + c // DECB, c % DECB, :].unsqueeze(0).to_broadcast([128, 512])).then_inc(v_in.sem, 16)
                        if w == 9:
                            sp.wait_ge(s_v.sem, s_v.at(l, V_DEC[0] + 8))
                            save_states(l, "ret_s")
                            sp.wait_ge(state_out, l * 64 + 32)
                            sp.wait_ge(so_ps.sem, so_ps.at(l, 1))
                            load_states(l, "state_gla")
                        if w == 19:
                            sp.wait_ge(s_v.sem, s_v.at(l, V_DEC[1] + 8))
                            save_states(l, "gla_s")
                if b == 0:
                    sp.wait_ge(s_v.sem, s_v.at(l, 0))
                    load_states(l, "state_ret")
                    save_v(l, 0)
                if b == NBLK - 1 and l < DEPTH - 1:
                    sp.wait_ge(gate_x.sem, gate_x.at(n, 2))
                    sp.wait_ge(s_v.sem, s_v.at(l, V_LAST))
                    load_par(l + 1)
                sp.wait_ge(st_ps.sem, st_ps.at(n, 8))
                src = d["x_prompt"] if l == 0 else d["acts"]
                for t in range(TPB):
                    window(n, 25 + t)
                    sp.dma_start(y_t[:, t, :], src[b * BLK + t * TOK:b * BLK + t * TOK + TOK, :]).then_inc(res_in.sem, 16)
                if b == 0:
                    save_v(l, 1)
                sp.wait_ge(sgla_sb.sem, sgla_sb.at(n, 9))
                sp.dma_start(fin_w, d["fin_w"]).then_inc(fin_in.sem, 16)
                if b == NBLK - 1:
                    sp.wait_ge(sret_sb.sem, sret_sb.at(n, 4))
                    sp.dma_start(d["ret_p"][l, :, :], s_ret[:, :]).then_inc(st_saved, 16)
                    sp.wait_ge(sgla_sb.sem, sgla_sb.at(n, 9))
                    sp.dma_start(d["gla_p"][l, :, :], s_gla[:, :]).then_inc(st_saved, 16)
                if n == (DEPTH - 1) * NBLK + 1:
                    sp.wait_ge(s_v.sem, s_v.at(l, V_LAST))
                    sp.wait_ge(state_out, l * 64 + 64)
                    sp.dma_start(d["y_sample"], ys).then_inc(fin_out, 16)
            for t in range(TPB):
                store_out(DEPTH * NBLK - 1, t)
            sp.wait_ge(x_in.sem, x_in.at(DEPTH * NBLK, 64))
            sp.wait_ge(nw_in.sem, nw_in.at(DEPTH * NBLK, 16))
            sp.wait_ge(fin_out, 16)
            sp.wait_ge(st_saved, 16 * 2 * DEPTH + 32)
            sp.wait_ge(state_out, 16 * 4 * DEPTH)
            sp.wait_ge(stored.sem, stored.at(DEPTH * NBLK, 0))

        @block.gpsimd
        def _(pool):
            pool.memset(half[:, :], -0.5).then_inc(sets, 1)
            pool.memset(spare[:, 31:32], 0.0).then_inc(sets, 1)
            pool.memset(z_u[:, 0:64], 0.0).then_inc(sets, 1)
            pool.memset(lr_s[:, :], 1.0).then_inc(sets, 1)
            pool.memset(a_gla[:, :, :], 0.0).then_inc(sets, 1)
            for c, (s, credit) in enumerate(((lo_done, RING), (slot_used, RING), (stored.sem, 16), (y_add.sem, 8), (st_saved, 32))):
                pool.memset(tmp[:, 0, c:c + 1], 0.0).then_inc(s, credit)
            pool.wait_ge(sets, 5)

            def rsqrt(dst, src, s):
                pool.tensor_tensor(dst, src, half[0:dst.shape[0], 0:dst.shape[-1]], ALU.pow).then_inc(s, 1)

            pool.wait_ge(xstat.sem, xstat.at(0, 4))
            rsqrt(xrs[:, :], xvar[:, :], rstd_x.sem)
            pool.wait_ge(s_v.sem, s_v.at(0, 4 - 6))
            rsqrt(srs[:, :], svar[:, :], s_p.sem)
            for h in range(2 * AHEAD):
                split_lo(pool, 0, h)

            with pool.Fori(0, DEPTH) as l:
                def body(n, next_row, kind):
                    for w in range(SLOTS):
                        split_lo(pool, n, 2 * (w + AHEAD))
                        split_lo(pool, n, 2 * (w + AHEAD) + 1)
                        for g, first in ((0, 10), (1, 22)):
                            t = w - first
                            if 0 <= t < TPB:
                                pool.wait_ge(ostat.sem, ostat.at(n, 3 * (t + 1) if g == 0 else 12 + 4 * (t + 1)))
                                rsqrt(rstd[:, t % 2, :], var[:, t % 2, :], rstd_o.sem)
                        if w == 19:
                            pool.wait_ge(xstat.sem, xstat.at(n + 1, 4))
                            rsqrt(xrs[:, :], xvar[:, :], rstd_x.sem)
                        if w in (22, 23, 24) and kind == 1:
                            pool.wait_ge(s_v.sem, s_v.at(l, V_VAR))
                            c = slice(22 * (w - 22), min(22 * (w - 22) + 22, 64))
                            rsqrt(rs_s[:, c], v_s[:, 0, c], s_p.sem)
                        if 15 <= w < 19:
                                t = w - 15
                                g = 4
                                pool.wait_ge(mhi_sb.sem, mhi_sb.at(n, t + 1))
                                pool.tensor_tensor(m_lo[:, g:g + 4, TOK * t:TOK * t + TOK], tmp[:, t % 2, :].rearrange("p (h n) -> p h n", h=4),
                                                   m_hi[:, g:g + 4, TOK * t:TOK * t + TOK].bitcast(f32), ALU.subtract).then_inc(mlo_sb.sem, 1)
                    pool.wait_ge(ystat.sem, ystat.at(n, 4))
                    rsqrt(yrs[:, :], xvar[:, :], rstd_y.sem)
                    if kind == 1:
                        pool.wait_ge(s_v.sem, s_v.at(l, V_NV))
                        rsqrt(srs[:, :], svar[:, :], s_p.sem)

                blocks(pool, l, body)

        @block.tensor
        def _(pe):
            pe.wait_ge(const_in, 144)

            for k in range(KT):
                next_transpose(pe, 0, k)
            with pe.Fori(0, DEPTH) as l:
                def body(n, next_row, kind):
                    def hT_slot0():
                        pe.wait_ge(hlo_sb.sem, hlo_sb.at(n, 8))
                        if kind == 0:
                            pe.wait_ge(s_v.sem, s_v.at(l, 0))
                            for k in range(KT):
                                i = pe.matmul(X[:, 8 * k:8 * k + 8], xsn[:, 128 * k:128 * k + 128], ident[0:8, 0:8], start=True, stop=True)
                            i.then_inc(xs_t.sem, 1)
                        wait_slot(pe, n, 0)
                        for k in range(KT):
                            for h in (h_hi, h_lo):
                                i = pe.matmul(ATT[0:32, :], w_gate[:, k, :], h[:, k, :], start=(k == 0 and h is h_hi), stop=(k == KT - 1 and h is h_lo))
                        if kind == 0:
                            pe.wait_ge(s_v.sem, s_v.at(l, V_H))
                            for k in range(KT):
                                i = pe.matmul(X[0:16, 256:288], hs[:, k, :], w_gate[:, k, :], start=(k == 0), stop=(k == KT - 1))
                        i.then_inc(slot_used, 1)

                    def unit_slot(u, s):
                        j = 1 + 4 * u + s
                        wait_slot(pe, n, j)
                        r = j % RING
                        natural = u in (1, 4, 6, 7)
                        for q in range(4):
                            if s == 0:
                                free_bank(u, q)
                            if u == 6 and s == 2:
                                pe.wait_ge(mlo_sb.sem, mlo_sb.at(n, 4 + q + 1))
                            for kk in range(2):
                                k = 2 * s + kk
                                if u >= 6:
                                    k = (k + 4) % 8
                                a_hi, a_lo = (m_hi, m_lo) if u >= 6 else (h_hi, h_lo)
                                if natural:
                                    cols = slice(512 * kk, 512 * kk + 512)
                                    tile = slice(TOK * q, TOK * q + TOK)
                                    prods = [(a_hi[:, k, tile], w_hi[:, r, cols]), (a_hi[:, k, tile], w_lo[:, r, cols]), (a_lo[:, k, tile], w_hi[:, r, cols])]
                                else:
                                    cols = slice(512 * kk + 128 * q, 512 * kk + 128 * q + 128)
                                    prods = [(w_hi[:, r, cols], a_hi[:, k, :]), (w_hi[:, r, cols], a_lo[:, k, :]), (w_lo[:, r, cols], a_hi[:, k, :])]
                                for c, (x, y) in enumerate(prods):
                                    i = pe.matmul(P[q][:, :], x, y, start=(s == 0 and kk == 0 and c == 0), stop=(s == 3 and kk == 1 and c == 2),
                                                  skip_group_check=True)
                            if q < 3 and s == 3:
                                i.then_inc(proj.sem, 1)
                        if kind == 0 and u < 6:
                            if s == 0:
                                free_sample_bank(u)
                            for kk in range(2):
                                for part in (w_hi, w_lo):
                                    i = pe.matmul((ST if Z_BANK[u] == "S" else X)[0:16, :], hs[:, 2 * s + kk, :], part[:, r, 512 * kk:512 * kk + 512],
                                                  start=(s == 0 and kk == 0 and part is w_hi), stop=(s == 3 and kk == 1 and part is w_lo))
                        if kind == 1 and u >= 6:
                            if u == 6 and s == 0:
                                pe.wait_ge(s_v.sem, s_v.at(l, V_MIX))
                                pe.wait_ge(o_sb.sem, o_sb.at(n, 8))
                            if u == 7 and s == 0:
                                pe.wait_ge(s_v.sem, s_v.at(l, V_X0))
                            for kk in range(2):
                                k = (2 * s + kk + 4) % 8
                                for part in (w_hi, w_lo):
                                    i = pe.matmul(OB[0:40, :], ms[:, k, :], part[:, r, 512 * kk:512 * kk + 512],
                                                  start=(s == 0 and kk == 0 and part is w_hi), stop=(s == 3 and kk == 1 and part is w_lo))
                        i.then_inc(slot_used, 1)

                    def free_sample_bank(u):
                        if u == 1:
                            pe.wait_ge(z_sb.sem, z_sb.at(l, 2))
                        elif u == 2:
                            pe.wait_ge(kn_sb.sem, kn_sb.at(n, 2))
                        elif u == 3:
                            pe.wait_ge(sret_sb.sem, sret_sb.at(n, 4))
                        elif u == 4:
                            pe.wait_ge(z_sb.sem, z_sb.at(l, 5))
                        elif u == 5:
                            pe.wait_ge(kn_sb.sem, kn_sb.at(n, 4))

                    def z_transposed(c, dst, columns, what):
                        pe.wait_ge(z_sb.sem, z_sb.at(l, what))
                        if what == 1:
                            i = pe.matmul(dst[0:64, c:c + 8], z_u[0:16, 0:64], comb[:, 0:8], start=True, stop=True)
                        for q in range(columns if what > 1 else 0):
                            i = pe.matmul(dst[:, c + 8 * q:c + 8 * q + 8], z_u[0:16, 128 * q:128 * q + 128], comb[:, 0:8], start=True, stop=True)
                        i.then_inc(zt_ps.sem, 1)

                    def v_natural():
                        pe.matmul(ATT[0:64, :], comb[:, :], z_v[:, :], start=True, stop=True).then_inc(vn_ps.sem, 1)

                    def sample_outputs(g):
                        pe.wait_ge(kn_sb.sem, kn_sb.at(n, 2 + 2 * g))
                        pe.wait_ge(s_v.sem, s_v.at(l, V_DEC[g] + 8))
                        for p in range(2):
                            for t in range(DECB):
                                c = 2 * (8 * p + t)
                                i = pe.matmul(X[:, c:c + 2], ss[:, p, t, :], q_s[:, g, p, t, :], start=True, stop=True)
                        i.then_inc(so_ps.sem, 1)

                    def sample_work(w):
                        if kind == 0:
                            if w == 1:
                                z_transposed(128, X, 1, 1)
                            if w == 2:
                                pe.wait_ge(zt_sb.sem, zt_sb.at(l, 1))
                                for q in range(2):
                                    i = pe.matmul(X[:, 144 + 8 * q:152 + 8 * q], w2b[0:2 * RANK + 1, 128 * q:128 * q + 128], lr_s[0:2 * RANK + 1, 0:8], start=True, stop=True)
                                i.then_inc(gx_ps.sem, 1)
                            if w == 6:
                                pe.wait_ge(em_sb.sem, em_sb.at(n, 1))
                                z_transposed(128, X, 4, 2)
                            if w == 13:
                                z_transposed(0, ATT, 4, 4)
                            if w == 14:
                                pe.wait_ge(zt_sb.sem, zt_sb.at(l, 3))
                                v_natural()
                            if w == 26:
                                pe.wait_ge(zt_sb.sem, zt_sb.at(l, 5))
                                v_natural()
                            if w == 17:
                                pe.wait_ge(vn_sb.sem, vn_sb.at(l, 1))
                                z_transposed(0, ATT, 4, 5)
                            if w == 25:
                                z_transposed(0, ATT, 4, 7)
                        if kind == 1:
                            if w == 10:
                                sample_outputs(0)
                            if w == 20:
                                sample_outputs(1)
                            if w == 21:
                                pe.wait_ge(s_v.sem, s_v.at(l, V_SQ))
                                pe.matmul(X[:, 128:256], ones[:, :], o_s[:, :, :].rearrange("p a n -> p (a n)"), start=True, stop=True).then_inc(mom_ps.sem, 1)

                    def free_bank(u, q):
                        if u == 0:
                            pe.wait_ge(y_add.sem, n * 8 + (4 + q + 1))
                        elif u == 1:
                            pe.wait_ge(q_raw.sem, q_raw.at(n, q + 1)) if q < 2 else pe.wait_ge(k_raw.sem, k_raw.at(n, q - 1))
                        elif u == 2:
                            pe.wait_ge(v_sb.sem, v_sb.at(n, q + 1))
                        elif u == 3:
                            pe.wait_ge(g_silu.sem, g_silu.at(n, q + 1))
                        elif u == 4:
                            pe.wait_ge(qk_gla.sem, qk_gla.at(n, q + 1))
                        elif u == 5:
                            pe.wait_ge(v_sb.sem, v_sb.at(n, 4 + q + 1))
                        elif u == 6:
                            pe.wait_ge(g_silu.sem, g_silu.at(n, 4 + q + 1))
                        else:
                            pe.wait_ge(y_add.sem, y_add.at(n, q + 1))

                    def keys_natural(g):
                        if g == 0:
                            pe.wait_ge(rope_st.sem, rope_st.at(n, 8))
                            pe.wait_ge(ex_sb.sem, ex_sb.at(n, 2))
                            pe.wait_ge(em_sb.sem, em_sb.at(n, 1))
                            if kind == 0:
                                pe.wait_ge(zt_sb.sem, zt_sb.at(l, 2))
                        else:
                            pe.wait_ge(qk_gla.sem, qk_gla.at(n, 4))
                            pe.wait_ge(m_aff.sem, m_aff.at(n, 4))
                            pe.wait_ge(att_sb.sem, att_sb.at(n, 4))
                            if kind == 0:
                                pe.wait_ge(zt_sb.sem, zt_sb.at(l, 4))
                        for t in range(TPB):
                            for p in range(2):
                                c = 256 * (t % 2) + 128 * p
                                i = pe.transpose((X, ATT)[t // 2][:, c:c + 128], k_t[:, p, TOK * t:TOK * t + TOK], ident[:, :])
                            if t % 2 == 1:
                                i.then_inc(kn_ps.sem, 1)

                    def scores(g, t):
                        tile = slice(TOK * t, TOK * t + TOK)
                        if g == 0 and t == 0:
                            pe.wait_ge(rope_st.sem, rope_st.at(n, 18))
                        if t == 0:
                            pe.wait_ge(kn_sb.sem, kn_sb.at(n, 2 * g + 2))
                        else:
                            pe.wait_ge(att_sb.sem, att_sb.at(n, 4 * g + t))
                        for p in range(2):
                            for hh in range(2):
                                h = 2 * p + hh
                                i = pe.matmul(ATT[:, 128 * h:128 * h + 128], k_t[:, p, tile], q_t[:, p, hh, tile], start=True, stop=True)
                        i.then_inc(att_ps.sem, 1)

                    def outputs(g, t):
                        tile = slice(TOK * t, TOK * t + TOK)
                        a, s = (a_ret, s_ret) if g == 0 else (a_gla, s_mid)
                        pe.wait_ge(att_sb.sem, att_sb.at(n, 4 * g + t + 1))
                        pe.wait_ge(v_sb.sem, v_sb.at(n, 4 * g + t + 1))
                        if g == 0 and t == 0:
                            pe.wait_ge(ex_sb.sem, ex_sb.at(n, 4))
                        if t == 0 and kind == 0:
                            pe.wait_ge(z_sb.sem, z_sb.at(l, 6 if g else 3))
                        if g + t > 0:
                            pe.wait_ge(o_sb.sem, o_sb.at(n, 4 * g + t))
                        if g == 0 and t > 0:
                            pe.wait_ge(sret_sb.sem, sret_sb.at(n, t))
                        if g == 1:
                            pe.wait_ge(sret_sb.sem, sret_sb.at(n, 4))
                            pe.wait_ge(sgla_sb.sem, sgla_sb.at(n, 1 + 2 * t))
                        for h in range(HEADS):
                            hc = slice(128 * h, 128 * h + 128)
                            pe.matmul(OB[:, hc], a[:, h, :], v_n[:, t, hc], start=True, stop=False)
                            i = pe.matmul(OB[:, hc], q_t[:, h // 2, h % 2, tile], s[:, hc], start=False, stop=True)
                        i.then_inc(o_ps.sem, 1)
                        for p in range(2):
                            i = pe.matmul(ST[:, 256 * p:256 * p + 256], k_n[:, t, 128 * p:128 * p + 128], v_n[:, t, 256 * p:256 * p + 256], start=True, stop=True)
                        i.then_inc(st_ps.sem, 1)

                    def mixed_t(g, t):
                        pe.wait_ge(normed.sem, normed.at(n, 4 * g + t + 1))
                        dst = X if g == 0 or t % 2 == 0 else ST
                        if g == 0:
                            pe.wait_ge(kn_sb.sem, kn_sb.at(n, 2)) if t == 0 else pe.wait_ge(m_aff.sem, m_aff.at(n, t))
                            if kind == 0:
                                pe.wait_ge(z_sb.sem, z_sb.at(l, 4))
                            if kind == 1:
                                pe.wait_ge(s_v.sem, s_v.at(l, V_O[0]))
                        elif t < 2:
                            pe.wait_ge(kn_sb.sem, kn_sb.at(n, 4))
                            pe.wait_ge(sgla_sb.sem, sgla_sb.at(n, 8))
                            if kind == 0:
                                pe.wait_ge(z_sb.sem, z_sb.at(l, 7))
                            if kind == 1:
                                pe.wait_ge(s_v.sem, s_v.at(l, V_MOM))
                        else:
                            pe.wait_ge(mix_sb.sem, mix_sb.at(n, 4 + t - 1))
                        for h in range(HEADS):
                            i = pe.transpose(dst[:, 128 * h:128 * h + 128], o_n[:, t, 128 * h:128 * h + 128], ident[:, :])
                        i.then_inc(mt_ps.sem, 1)

                    hT_slot0()
                    sample_work(0)
                    for w in range(1, SLOTS):
                        u, s = (w - 1) // 4, (w - 1) % 4
                        if u == 6 and s == 0:
                            pe.wait_ge(mlo_sb.sem, mlo_sb.at(n, 4))
                        unit_slot(u, s)
                        if w == 1:
                            for hf, dst in ((0, ATT), (1, OB)):
                                if hf == 0:
                                    pe.wait_ge(lr_sb.sem, lr_sb.at(n, 1))
                                elif kind == 2:
                                    pe.wait_ge(s_v.sem, s_v.at(l, V_X1))
                                for t2 in range(2):
                                    t = 2 * hf + t2
                                    i = pe.matmul(dst[:, 256 * t2:256 * t2 + 256], lr_t[0:2 * RANK + 1, TOK * t:TOK * t + TOK], w2b[:, :], start=True, stop=True)
                                i.then_inc(gate_x.sem, 1)
                        if w == 4:
                            for p, dst in ((0, ATT), (1, OB)):
                                pe.wait_ge(la_sb.sem, la_sb.at(n, 2))
                                for t in range(TPB):
                                    i = pe.matmul(dst[:, TOK * t:TOK * t + TOK], la[:, t, 128 * p:128 * p + 128], cum[:, 0:128], start=True, stop=True)
                                i.then_inc(cum_b.sem, 1)
                            if kind == 0:
                                pe.wait_ge(s_v.sem, s_v.at(l, V_LA))
                            for t in range(TPB):
                                for p in range(2):
                                    c = 4 * t + 2 * p
                                    i = pe.matmul(X[:, c:c + 2], la[:, t, 128 * p:128 * p + 128], cum[:, 128:130], start=True, stop=True)
                            i.then_inc(mid_b.sem, 1)
                        if w in (7, 19):
                            keys_natural(w // 19)
                        for g, first in ((0, 8), (1, 20)):
                            t = w - first
                            if 1 <= t <= TPB:
                                outputs(g, t - 1)
                            if 0 <= t < TPB:
                                scores(g, t)
                        if 13 <= w < 17:
                            mixed_t(0, w - 13)
                        if w in (25, 26):
                            mixed_t(1, 2 * (w - 25))
                            mixed_t(1, 2 * (w - 25) + 1)
                        if 27 <= w < 31:
                            for k in (2 * (w - 27), 2 * (w - 27) + 1):
                                if k == 0:
                                    pe.wait_ge(mix_sb.sem, mix_sb.at(n, 7))
                                if k == 1:
                                    pe.wait_ge(att_sb.sem, att_sb.at(n, 8))
                                    if kind == 0:
                                        pe.wait_ge(vn_sb.sem, vn_sb.at(l, 2))
                                next_transpose(pe, n + 1, k)
                        sample_work(w)

                blocks(pe, l, body)

        @block.scalar
        def _(act):
            act.wait_ge(sets, 5)
            load_half(act, 0, 0, 0)
            load_half(act, 0, 0, 1)
            for h in range(2 * AHEAD):
                split_hi(act, 0, h)
                load_half(act, 0, 0, h + 2)
            for k in range(KT):
                next_hi(act, 0, k)
            with act.Fori(0, DEPTH) as l:
                def body(n, next_row, kind):
                    def z_out(w):
                        u = Z_READ.index(w)
                        if u in (2, 3, 5):
                            act.wait_ge(zt_ps.sem, zt_ps.at(l, {2: 2, 3: 3, 5: 4}[u]))
                        elif u == 0:
                            act.wait_ge(zt_ps.sem, zt_ps.at(l, 1))
                        elif u == 4:
                            act.wait_ge(v_out, l * 32 + 16)
                        act.wait_ge(slot_used, n * SLOTS + (w + RING))
                        dst = z_v if u in (1, 4) else z_u
                        nc.scalar.activation(dst, (ST if Z_BANK[u] == "S" else X)[0:16, :], ACT.Copy).then_inc(z_sb.sem, 1)

                    def sample_work(w):
                        if kind == 1 or kind == 2:
                            return
                        if w == 1:
                            act.wait_ge(slot_used, n * SLOTS + (1 + RING))
                            nc.scalar.activation(z_u[:, 0:32], X[0:16, 256:288], ACT.Copy).then_inc(z_sb.sem, 1)
                        if w == 2:
                            act.wait_ge(zt_ps.sem, zt_ps.at(l, 1))
                            nc.scalar.activation(lr_s[0:32, :], X[0:32, 128:136], ACT.Copy).then_inc(zt_sb.sem, 1)
                        if w == 3:
                            act.wait_ge(gx_ps.sem, gx_ps.at(l, 1))
                            nc.scalar.activation(gt[:, :], X[:, 144:160], ACT.Abs).then_inc(gl_s.sem, 1)
                            act.wait_ge(gl_s.sem, gl_s.at(l, 1))
                            nc.scalar.activation(gt[:, :], gt[:, :], ACT.Exp, scale=-1.0).then_inc(gl_s.sem, 1)
                            act.wait_ge(gl_s.sem, gl_s.at(l, 2))
                            nc.scalar.activation(gt[:, :], gt[:, :], ACT.Ln, bias=1.0).then_inc(gl_s.sem, 1)
                        if w in (15, 27):
                            act.wait_ge(vn_ps.sem, vn_ps.at(l, 1 + w // 27))
                            nc.scalar.activation(z_v[0:8, :], ATT[0:8, :], ACT.Copy).then_inc(vn_sb.sem, 1)
                        if w in (7, 14, 18, 26):
                            c = (7, 14, 18, 26).index(w)
                            act.wait_ge(zt_ps.sem, zt_ps.at(l, c + 2))
                            nc.scalar.activation(z_t[:, 4 * c:4 * c + 4, :], (X[:, 128:160] if c == 0 else ATT[:, 0:32]).rearrange("p (a b) -> p a b", b=8),
                                                 ACT.Copy).then_inc(zt_sb.sem, 1)
                        if w == 7:
                            act.wait_ge(s_v.sem, s_v.at(l, V_LA))
                            nc.scalar.activation(al[:, :], al[:, :], ACT.Exp, scale=1.0 / TAU).then_inc(al_s.sem, 1)
                        if w == 27:
                            act.wait_ge(zt_sb.sem, zt_sb.at(l, 5))
                            for g in range(2):
                                nc.scalar.activation(sg_s[:, 32 * g:32 * g + 32].rearrange("p (a b) -> p a b", b=8), z_t[:, 4 + 8 * g:8 + 8 * g, :],
                                                     ACT.Tanh, scale=0.5).then_inc(tg_s.sem, 1)

                    for w in range(SLOTS):
                        if w == 1:
                            act.wait_ge(slot_used, n * SLOTS + (1 + RING))
                            act.wait_ge(lr_ones.sem, lr_ones.at(n, 1))
                            nc.scalar.activation(lr_t[0:2 * RANK, :], ATT[0:2 * RANK, :], ACT.Copy).then_inc(lr_sb.sem, 1)
                        if w == 5:
                            for q in range(2):
                                if q == 0:
                                    act.wait_ge(stored.sem, stored.at(n, 0))
                                wait_bank(act, n, 0, 2 + q)
                                nc.scalar.activation(k_t[:, q, :], P[2 + q][:, :], ACT.Copy).then_inc(k_raw.sem, 1)
                        if w in (9, 21):
                            g = w // 21
                            for q in range(4):
                                wait_bank(act, n, 1 + 3 * g, q)
                                nc.scalar.activation(v_n[:, q, :], P[q][:, :], ACT.Copy).then_inc(v_sb.sem, 1)
                        if w in (13, 25):
                            g = w // 25
                            if g == 1:
                                act.wait_ge(mix_sb.sem, mix_sb.at(n, 4))
                            for q in range(4):
                                wait_bank(act, n, 2 + 3 * g, q)
                                nc.scalar.activation(g_t[:, q, :], P[q][:, :], ACT.Tanh, scale=0.5).then_inc(g_tanh.sem, 1)
                        if kind == 0 and w in Z_READ:
                            z_out(w)
                        for h in (2 * (w + AHEAD), 2 * (w + AHEAD) + 1):
                            split_hi(act, n, h)
                            load_half(act, l * SLOTS if h + 2 < 2 * SLOTS else next_row - SLOTS, n, h + 2)
                        sample_work(w)
                        if w == 2:
                            for hf, src in ((0, ATT), (1, OB)):
                                act.wait_ge(gate_x.sem, gate_x.at(n, hf + 1))
                                nc.scalar.activation(tmp[:, hf, :], src[:, :], ACT.Abs).then_inc(gate_l.sem, 1)
                                act.wait_ge(gate_l.sem, gate_l.at(n, 3 * hf + 1))
                                nc.scalar.activation(tmp[:, hf, :], tmp[:, hf, :], ACT.Exp, scale=-1.0).then_inc(gate_l.sem, 1)
                                act.wait_ge(gate_l.sem, gate_l.at(n, 3 * hf + 2))
                                nc.scalar.activation(tmp[:, hf, :], tmp[:, hf, :], ACT.Ln, bias=1.0).then_inc(gate_l.sem, 1)
                        if w == 6:
                            for p, src in ((0, ATT), (1, OB)):
                                act.wait_ge(cum_b.sem, cum_b.at(n, p + 1))
                                for sgn in range(2):
                                    nc.scalar.activation(ex[:, p, sgn, :], src[:, :], ACT.Exp, scale=1.0 - 2.0 * sgn).then_inc(ex_sb.sem, 1)
                            act.wait_ge(mid_b.sem, mid_b.at(n, 1))
                            nc.scalar.activation(em[:, :, :, :].rearrange("p a b c -> p (a b c)"), X[:, 0:16], ACT.Exp).then_inc(em_sb.sem, 1)
                        for g, first in ((0, 10), (1, 22)):
                            t = w - first
                            if 0 <= t < TPB:
                                act.wait_ge(o_ps.sem, o_ps.at(n, 4 * g + t + 1))
                                nc.scalar.activation(o_n[:, t, :], OB[:, :], ACT.Copy).then_inc(o_sb.sem, 1)
                        if 14 <= w < 18:
                            t = w - 14
                            act.wait_ge(mt_ps.sem, mt_ps.at(n, t + 1))
                            if t >= 2:
                                act.wait_ge(mlo_sb.sem, mlo_sb.at(n, t - 1))
                            for h in range(HEADS):
                                i = nc.scalar.activation(tmp[:, t % 2, 128 * h:128 * h + 128], X[:, 128 * h:128 * h + 128], ACT.Identity,
                                                         scale=parh[:, 1 + h:2 + h], bias=parh[:, 5 + h:6 + h])
                            i.then_inc(m_aff.sem, 1)
                        if 15 <= w < 19:
                            t = w - 15
                            act.wait_ge(mix_sb.sem, mix_sb.at(n, t + 1))
                            nc.scalar.activation(m_hi[:, 4:8, TOK * t:TOK * t + TOK], tmp[:, t % 2, :].rearrange("p (h n) -> p h n", h=4), ACT.Copy).then_inc(mhi_sb.sem, 1)
                        if 28 <= w < 32:
                            next_hi(act, n + 1, 2 * (w - 28))
                            next_hi(act, n + 1, 2 * (w - 28) + 1)
                blocks(act, l, body)
            for h in (2 * (SLOTS + AHEAD), 2 * (SLOTS + AHEAD) + 1):
                act.wait_ge(w_loaded[h % RING], (DEPTH * NBLK - 1) * (2 * SLOTS // RING * 16) + (h // RING + 1) * 16)

        @block.vector
        def _(vec):
            next_stats(vec, 0, first=True)
            vec.wait_ge(const_in, 144)
            vec.wait_ge(sets, 5)

            def step(i):
                i.then_inc(s_v.sem, 1)

            def sample_stats(l, k):
                for s in range(2):
                    i = vec.bn_stats(sbn[:, 6 * s:6 * s + 6], xs[:, 512 * s:512 * s + 512])
                step(i)
                vec.wait_ge(s_v.sem, s_v.at(l, k + 1))
                apart()
                step(vec.bn_aggr(sagg[:, :], sbn[:, :]))
                vec.wait_ge(s_v.sem, s_v.at(l, k + 2))
                step(vec.tensor_tensor(smsq[:, :], sagg[:, 0:1], sagg[:, 0:1], ALU.mult))
                vec.wait_ge(s_v.sem, s_v.at(l, k + 3))
                step(vec.scalar_tensor_tensor(svar[:, :], smsq[:, :], EPS, sagg[:, 1:2], ALU.add, ALU.add))

            def sample_norm(l, first):
                if first:
                    vec.wait_ge(s_p.sem, s_p.at(l, 0))
                    step(vec.tensor_scalar(xsn[:, :], xs[:, :], srs[:, :], None, ALU.mult))
                    step(vec.memset(spare[:, 30:31], 0.0))
                else:
                    vec.wait_ge(s_p.sem, s_p.at(l, 4))
                    vec.wait_ge(v_out, l * 32 + 32)
                    vec.wait_ge(state_out, l * 64 + 64)
                    step(vec.tensor_scalar(xsn[:, :], xs[:, :], srs[:, :], None, ALU.mult))
                    step(vec.scalar_tensor_tensor(ys[:, :], xs[:, :], srs[:, :], fin_w[0:8, :], ALU.mult, ALU.mult))

            vec.tensor_scalar(gmask[:, :], rmask[:, 0:TOK], 0.0, None, ALU.is_gt)
            vec.memset(lr_t, 1.0).then_inc(lr_ones.sem, 1)
            vec.tensor_copy(ms[:, :, 8:32], spare[:, 31:32].unsqueeze(2).to_broadcast([128, KT, 24]))
            sample_stats(0, -6)
            next_norm(vec, 0)
            sample_norm(0, True)
            for k in range(KT):
                next_lo(vec, 0, k)
            with vec.Fori(0, DEPTH) as l:
                def body(n, next_row, kind):
                    def done(k):
                        vec.wait_ge(s_v.sem, s_v.at(l, k))

                    def sample_start():
                        vec.wait_ge(par_in, l * 32 + 32)
                        vec.wait_ge(xs_t.sem, xs_t.at(l, 1))
                        hs_v = hs_f[:, :].rearrange("p (k b) -> p k b", b=8)
                        step(vec.tensor_tensor(hs_v, X[:, 0:64].rearrange("p (k b) -> p k b", b=8),
                                               par[:, 0:8].unsqueeze(2).to_broadcast([128, 8, 8]), ALU.mult))
                        done(1)
                        step(vec.tensor_copy(hs[:, :, 0:8], hs_v))
                        done(2)
                        step(vec.tensor_tensor(hs[:, :, 8:16], hs_v, hs[:, :, 0:8].bitcast(f32), ALU.subtract))
                        vec.tensor_scalar(parh[:, :], par[:, 8:17], 0.5, None, ALU.mult)
                        vec.wait_ge(st_saved, l * 32 + 32)
                        vec.memset(s_ret[:, :], 0.0)
                        vec.memset(s_gla[:, :], 0.0)

                    def sample_gate():
                        vec.wait_ge(gl_s.sem, gl_s.at(l, 3))
                        step(vec.scalar_tensor_tensor(al[:, :], X[:, 144:160], 0.0, gt[:, :], ALU.min, ALU.subtract))

                    def sample_q_ret():
                        vec.wait_ge(zt_sb.sem, zt_sb.at(l, 2))
                        step(vec.memset(q_s[:, :, :, :, :], 0.0))
                        done(5)
                        apart()
                        step(vec.stream_shuffle(rot[:, :, :], z_t[:, 0:4, :], [(p + 16) % 32 for p in range(32)]))
                        done(6)
                        vec.tensor_scalar(z_t[:, 0:2, :], z_t[:, 0:2, :], small[:, 0:1], None, ALU.mult)
                        step(vec.tensor_scalar(z_t[:, 2:4, :], z_t[:, 2:4, :], small[:, 2:3], None, ALU.mult))
                        done(7)
                        vec.scalar_tensor_tensor(rot[:, 0:2, :], rot[:, 0:2, :], small[:, 1:2], z_t[:, 0:2, :], ALU.mult, ALU.add)
                        step(vec.scalar_tensor_tensor(rot[:, 2:4, :], rot[:, 2:4, :], small[:, 3:4], z_t[:, 2:4, :], ALU.mult, ALU.add))
                        done(8)
                        for hh in range(2):
                            r = slice(64 * hh, 64 * hh + 64)
                            vec.tensor_copy(q_s[r, 0, :, :, hh], rot[r, 0:2, :])
                        step(vec.tensor_copy(k_s[:, 0, :, :], rot[:, 2:4, :]))

                    def sample_q_gla():
                        vec.wait_ge(zt_sb.sem, zt_sb.at(l, 4))
                        for hh in range(2):
                            r = slice(64 * hh, 64 * hh + 64)
                            vec.tensor_scalar(q_s[r, 1, :, :, hh], z_t[r, 8:10, :], DK ** -0.5, None, ALU.mult)
                        step(vec.tensor_copy(k_s[:, 1, :, :], z_t[:, 10:12, :]))

                    def sample_decay(g):
                        vec.wait_ge(state_in, l * 64 + 32 * g + 32)
                        if g == 0:
                            for p in range(2):
                                i = vec.tensor_scalar(ss[:, p, :, :], ss[:, p, :, :], small[:, 4 + p:5 + p], None, ALU.mult)
                            step(i)
                        else:
                            vec.wait_ge(al_s.sem, al_s.at(l, 1))
                            s2 = ss[:, :, :, :].rearrange("p i b n -> p (i b) n")
                            step(vec.tensor_tensor(s2, s2, al[:, :].unsqueeze(2).to_broadcast([128, 16, 128]), ALU.mult))

                    def sample_update(c):
                        g, t = c // DECB, c % DECB
                        if t == 0:
                            done(V_DEC[g])
                        vec.wait_ge(v_in.sem, v_in.at(l, 16 * c + 16))
                        for p in range(2):
                            for hh in range(2):
                                r, h = slice(64 * hh, 64 * hh + 64), 2 * p + hh
                                i = vec.scalar_tensor_tensor(ss[r, p, t, :], v_b[r, 128 * h:128 * h + 128], k_s[r, g, p, t:t + 1], ss[r, p, t, :], ALU.mult, ALU.add)
                        step(i)

                    def sample_o(g):
                        vec.wait_ge(so_ps.sem, so_ps.at(l, g + 1))
                        for hh in range(2):
                            i = vec.tensor_copy(o_s[:, 0, 32 * g:32 * g + 32].rearrange("p (a h b) -> p a h b", a=2, h=2)[:, :, hh, :],
                                                X[:, 0:32].rearrange("p (a b h) -> p a b h", a=2, h=2)[:, :, :, hh])
                        step(i)

                    def sample_moments():
                        done(30)
                        step(vec.tensor_tensor(o_s[:, 1, :], o_s[:, 0, :], o_s[:, 0, :], ALU.mult))

                    def sample_variance():
                        vec.wait_ge(mom_ps.sem, mom_ps.at(l, 1))
                        step(vec.tensor_copy(v_s[:, 1, :], X[:, 128:192]))
                        done(32)
                        step(vec.tensor_tensor(v_s[:, 0, 0:32], v_s[:, 1, 0:32], v_s[:, 1, 0:32], ALU.mult))
                        done(33)
                        vec.tensor_scalar(v_s[:, 0, 32:64], X[:, 224:256], EPS, None, ALU.add)
                        step(vec.tensor_tensor(v_s[:, 0, 0:32], X[:, 192:224], v_s[:, 0, 0:32], ALU.subtract))
                        done(34)
                        step(vec.tensor_scalar(v_s[:, 0, 0:32], v_s[:, 0, 0:32], 0.0, GN_EPS, ALU.max, ALU.add))
                        step(vec.tensor_tensor(o_s[:, 0, 0:32], o_s[:, 0, 0:32], v_s[:, 1, 0:32], ALU.subtract))

                    def sample_mixed():
                        done(36)
                        vec.wait_ge(s_p.sem, s_p.at(l, 3))
                        step(vec.tensor_tensor(o_s[:, 0, :], o_s[:, 0, :], rs_s[:, :], ALU.mult))
                        done(37)
                        for h in range(HEADS):
                            c = slice(8 * h, 8 * h + 8)
                            vec.tensor_scalar(o_s[:, 0, c], o_s[:, 0, c], parh[:, 1 + h:2 + h], parh[:, 5 + h:6 + h], ALU.mult, ALU.add)
                        step(vec.tensor_scalar(o_s[:, 0, 32:64], o_s[:, 0, 32:64], parh[:, 0:1], None, ALU.mult))
                        vec.wait_ge(tg_s.sem, tg_s.at(l, 2))
                        for g in range(2):
                            sv = sg_s[:, 32 * g:32 * g + 32].rearrange("p (a b) -> p a b", b=8)
                            i = vec.scalar_tensor_tensor(sv, sv, 1.0, z_t[:, 4 + 8 * g:8 + 8 * g, :], ALU.add, ALU.mult)
                        step(i)
                        done(39)
                        step(vec.tensor_tensor(o_s[:, 0, :], o_s[:, 0, :], sg_s[:, :], ALU.mult))
                        done(40)
                        o3 = o_s[:, 0, :].rearrange("p (c b) -> p c b", b=8)
                        vec.tensor_copy(ms[:, 4:8, 0:8], o3[:, 0:4, :])
                        step(vec.tensor_copy(ms[:, 0:4, 0:8], o3[:, 4:8, :]))
                        done(41)
                        vec.tensor_tensor(ms[:, 4:8, 32:40], o3[:, 0:4, :], ms[:, 4:8, 0:8].bitcast(f32), ALU.subtract)
                        step(vec.tensor_tensor(ms[:, 0:4, 32:40], o3[:, 4:8, :], ms[:, 0:4, 0:8].bitcast(f32), ALU.subtract))

                    def sample_residual(u):
                        vec.wait_ge(slot_used, n * SLOTS + (4 * (6 + u) + 5 + RING))
                        c = slice(512 * u, 512 * u + 512)
                        step(vec.tensor_tensor(xs[:, c], OB[0:8, :], xs[:, c], ALU.add))
                        done(43 + 2 * u)
                        step(vec.tensor_tensor(xs[:, c], OB[32:40, :], xs[:, c], ALU.add))

                    def sample_work(w):
                        if kind == 0:
                            if w == 4:
                                sample_gate()
                            if w == 8:
                                sample_q_ret()
                            if w == 19:
                                sample_q_gla()
                        if kind == 1:
                            if w == 1:
                                sample_decay(0)
                            if w == 12:
                                sample_decay(1)
                            if w - 1 in V_AT:
                                sample_update(V_AT.index(w - 1))
                            if w == 11:
                                sample_o(0)
                            if w == 21:
                                sample_o(1)
                                sample_moments()
                            if w == 29:
                                sample_residual(0)

                    def keys(g):
                        for hf, src in ((0, X), (1, ATT)):
                            vec.wait_ge(kn_ps.sem, kn_ps.at(n, 2 * g + hf + 1))
                            dst = k_n[:, 2 * hf:2 * hf + 2, :]
                            if g == 0:
                                vec.tensor_tensor(dst.rearrange("p t (h n) -> p t h n", h=HEADS), src[:, :].rearrange("p (t h n) -> p t h n", t=2, h=HEADS),
                                                  kdec[:, :].unsqueeze(1).unsqueeze(3).to_broadcast([128, 2, HEADS, DK]), ALU.mult).then_inc(kn_sb.sem, 1)
                            else:
                                vec.tensor_copy(dst, src[:, :].rearrange("p (t n) -> p t n", t=2)).then_inc(kn_sb.sem, 1)

                    def scores(g, t):
                        vec.wait_ge(att_ps.sem, att_ps.at(n, 4 * g + t + 1))
                        a3 = ATT[:, :].rearrange("p (h n) -> p h n", h=HEADS)
                        if g == 0:
                            vec.tensor_tensor(a_ret[:, :, :], a3, rmask[:, :].rearrange("p (h n) -> p h n", h=HEADS), ALU.mult).then_inc(att_sb.sem, 1)
                        else:
                            apart()
                            vec.copy_predicated(a_gla[:, :, :], gmask[:, :].unsqueeze(1).to_broadcast([128, HEADS, TOK]), a3).then_inc(att_sb.sem, 1)

                    def state(g, t):
                        vec.wait_ge(st_ps.sem, st_ps.at(n, 4 * g + t + 1))
                        if g == 0:
                            if t > 0:
                                vec.wait_ge(sret_sb.sem, sret_sb.at(n, t))
                            for p in range(2):
                                c = slice(256 * p, 256 * p + 256)
                                i = vec.scalar_tensor_tensor(s_ret[:, c], s_ret[:, c], small[:, 6 + p:7 + p], ST[:, c], ALU.mult, ALU.add)
                            i.then_inc(sret_sb.sem, 1)
                            return
                        vec.wait_ge(sgla_sb.sem, sgla_sb.at(n, 1 + 2 * t))
                        vec.tensor_tensor(s_gla[:, :], ST[:, :], s_mid[:, :], ALU.add).then_inc(sgla_sb.sem, 1)
                        vec.wait_ge(sgla_sb.sem, sgla_sb.at(n, 2 + 2 * t))
                        for p in range(2):
                            c = slice(256 * p, 256 * p + 256)
                            if t < TPB - 1:
                                i = vec.tensor_scalar(s_mid[:, c], s_gla[:, c], cc[:, p, t:t + 1], None, ALU.mult)
                            else:
                                i = vec.tensor_scalar(s_gla[:, c], s_gla[:, c], ex[:, p, 0, BLK - 1:BLK], None, ALU.mult)
                        i.then_inc(sgla_sb.sem, 1)

                    def stats(g, t):
                        z, base = t % 2, 3 * t if g == 0 else 12 + 4 * t
                        vec.wait_ge(o_sb.sem, o_sb.at(n, 4 * g + t + 1))
                        for h in range(HEADS):
                            i = vec.bn_stats(bns[:, z, h, :], o_n[:, t, 128 * h:128 * h + 128])
                        i.then_inc(ostat.sem, 1)
                        vec.wait_ge(ostat.sem, ostat.at(n, base + 1))
                        apart()
                        for h in range(HEADS):
                            i = vec.bn_aggr(agg[:, z, h, :], bns[:, z, h, :])
                        i.then_inc(ostat.sem, 1)
                        vec.wait_ge(ostat.sem, ostat.at(n, base + 2))
                        if g == 0:
                            vec.tensor_scalar(var[:, z, :], agg[:, z, :, 1], GN_EPS, None, ALU.add).then_inc(ostat.sem, 1)
                        else:
                            vec.tensor_tensor(msq[:, z, :], agg[:, z, :, 0], agg[:, z, :, 0], ALU.mult).then_inc(ostat.sem, 1)
                            vec.wait_ge(ostat.sem, ostat.at(n, base + 3))
                            vec.scalar_tensor_tensor(var[:, z, :], msq[:, z, :], EPS, agg[:, z, :, 1], ALU.add, ALU.add).then_inc(ostat.sem, 1)

                    def norm(g, t):
                        z = t % 2
                        vec.wait_ge(rstd_o.sem, rstd_o.at(n, 4 * g + t + 1))
                        for h in range(HEADS):
                            oh = o_n[:, t, 128 * h:128 * h + 128]
                            if g == 0:
                                i = vec.tensor_scalar(oh, oh, agg[:, z, h, 0:1], rstd[:, z, h:h + 1], ALU.subtract, ALU.mult)
                            else:
                                i = vec.tensor_scalar(oh, oh, rstd[:, z, h:h + 1], None, ALU.mult)
                        i.then_inc(normed.sem, 1)

                    def silu(g):
                        for q in range(4):
                            vec.wait_ge(g_tanh.sem, g_tanh.at(n, 4 * g + q + 1))
                            vec.scalar_tensor_tensor(g_t[:, q, :], g_t[:, q, :], 1.0, P[q][:, :], ALU.add, ALU.mult).then_inc(g_silu.sem, 1)

                    def mixed(g, t):
                        gate = g_t[:, :, TOK * t:TOK * t + TOK]
                        dst = tmp[:, t % 2, :].rearrange("p (h n) -> p h n", h=HEADS)
                        if g == 0:
                            vec.wait_ge(m_aff.sem, m_aff.at(n, t + 1))
                            if t == 0:
                                vec.wait_ge(g_silu.sem, g_silu.at(n, 4))
                            vec.tensor_tensor(dst, dst, gate, ALU.mult).then_inc(mix_sb.sem, 1)
                        else:
                            vec.wait_ge(mt_ps.sem, mt_ps.at(n, 4 + t + 1))
                            if t == 0:
                                vec.wait_ge(g_silu.sem, g_silu.at(n, 8))
                            vec.wait_ge(mlo_sb.sem, mlo_sb.at(n, 4 + t - 1 if t >= 2 else 4))
                            src = (X if t % 2 == 0 else ST)[:, :].rearrange("p (h n) -> p h n", h=HEADS)
                            vec.scalar_tensor_tensor(dst, src, parh[:, 0:1], gate, ALU.mult, ALU.mult).then_inc(mix_sb.sem, 1)
                            tile = slice(TOK * t, TOK * t + TOK)
                            vec.wait_ge(mix_sb.sem, mix_sb.at(n, 4 + t + 1))
                            vec.tensor_copy(m_hi[:, 0:4, tile], dst).then_inc(mhi_sb.sem, 1)
                            vec.wait_ge(mhi_sb.sem, mhi_sb.at(n, 4 + t + 1))
                            vec.tensor_tensor(m_lo[:, 0:4, tile], dst, m_hi[:, 0:4, tile].bitcast(f32), ALU.subtract).then_inc(mlo_sb.sem, 1)

                    def rotate():
                        for p in range(2):
                            wait_bank(vec, n, 0, p)
                            if p == 0:
                                vec.wait_ge(stored.sem, stored.at(n, 0))
                            q4 = [a.rearrange("p (t n) -> p t n", t=TPB) for a in (q_t[:, p, 0, :], P[p][:, :])]
                            vec.tensor_tensor(q4[0], q4[1], qdec[:, p, :].unsqueeze(1).to_broadcast([128, TPB, TOK]), ALU.mult).then_inc(q_raw.sem, 1)
                        vec.wait_ge(rope_in.sem, rope_in.at(n, 16))
                        vec.wait_ge(la_sb.sem, la_sb.at(n, 2))
                        c = 0
                        for i_ in (2, 3, 0, 1):
                            buf = q_t[:, i_, 0, :] if i_ < 2 else k_t[:, i_ - 2, :]
                            if i_ < 2:
                                vec.wait_ge(q_raw.sem, q_raw.at(n, i_ + 1))
                            else:
                                vec.wait_ge(k_raw.sem, k_raw.at(n, i_ - 1))
                            if c > 0:
                                vec.wait_ge(rope_st.sem, rope_st.at(n, c))
                            apart()
                            vec.stream_shuffle(r_tmp[:, :], buf, [(p + 16) % 32 for p in range(32)]).then_inc(rope_st.sem, 1)
                            vec.wait_ge(rope_st.sem, rope_st.at(n, c + 1))
                            vec.tensor_tensor(buf, buf, rope[:, 0, :], ALU.mult).then_inc(rope_st.sem, 1)
                            vec.wait_ge(rope_st.sem, rope_st.at(n, c + 2))
                            vec.tensor_tensor(r_tmp[:, :], r_tmp[:, :], rope[:, 1, :], ALU.mult).then_inc(rope_st.sem, 1)
                            vec.wait_ge(rope_st.sem, rope_st.at(n, c + 3))
                            if i_ < 2:
                                vec.memset(q_t[0:64, i_, 1, :], 0.0)
                                vec.tensor_tensor(q_t[64:128, i_, 1, :], buf[64:128, :], r_tmp[64:128, :], ALU.add)
                                vec.tensor_tensor(buf[0:64, :], buf[0:64, :], r_tmp[0:64, :], ALU.add).then_inc(rope_st.sem, 1)
                                vec.wait_ge(rope_st.sem, rope_st.at(n, c + 4))
                                vec.memset(buf[64:128, :], 0.0).then_inc(rope_st.sem, 1)
                                c += 5
                            else:
                                vec.tensor_tensor(buf, buf, r_tmp[:, :], ALU.add).then_inc(rope_st.sem, 1)
                                c += 4

                    if kind == 0:
                        sample_start()
                    for w in range(1, SLOTS):
                        if w in (3, 4):
                            hf = w - 3
                            vec.wait_ge(gate_l.sem, gate_l.at(n, 3 * hf + 3))
                            vec.scalar_tensor_tensor(la[:, 2 * hf:2 * hf + 2, :].rearrange("p a n -> p (a n)"), (ATT, OB)[hf][:, :], 0.0, tmp[:, hf, :],
                                                     ALU.min, ALU.subtract).then_inc(la_sb.sem, 1)
                        if w == 5:
                            rotate()
                        if w == 8:
                            vec.wait_ge(ex_sb.sem, ex_sb.at(n, 4))
                            vec.wait_ge(em_sb.sem, em_sb.at(n, 1))
                            for p in range(2):
                                i = vec.tensor_tensor(cc[:, p, 0:TPB - 1], ex[:, p, 0, TOK - 1:BLK - TOK:TOK], em[:, 1:TPB, p, 0], ALU.mult)
                            i.then_inc(cc_sb.sem, 1)
                            for p in range(2):
                                c = slice(256 * p, 256 * p + 256)
                                i = vec.tensor_scalar(s_mid[:, c], s_gla[:, c], em[:, 0, p, 0:1], None, ALU.mult)
                            i.then_inc(sgla_sb.sem, 1)
                        if w == 13:
                            silu(0)
                        if w == 17:
                            for p in range(2):
                                wait_bank(vec, n, 3, p)
                                for hh in range(2):
                                    r = slice(64 * hh, 64 * hh + 64)
                                    i = vec.scalar_tensor_tensor(q_t[r, p, hh, :], P[p][r, :], DK ** -0.5, ex[r, p, 0, :], ALU.mult, ALU.mult)
                                i.then_inc(qk_gla.sem, 1)
                            for p in range(2):
                                wait_bank(vec, n, 3, 2 + p)
                                vec.tensor_tensor(k_t[:, p, :], P[2 + p][:, :], ex[:, p, 1, :], ALU.mult).then_inc(qk_gla.sem, 1)
                        if w == 25:
                            silu(1)
                        if w in (8, 20):
                            keys(w // 20)
                        if w == 22 and kind == 1:
                            sample_variance()
                        for g, first in ((0, 9), (1, 21)):
                            t = w - first
                            if 0 <= t < TPB:
                                scores(g, t)
                            if 1 <= t <= TPB:
                                state(g, t - 1)
                            if 2 <= t <= TPB + 1:
                                norm(g, t - 2)
                            if w == 25 and g == 1 and kind == 1:
                                sample_mixed()
                            if 1 <= t <= TPB:
                                stats(g, t - 1)
                        if 14 <= w < 18:
                            mixed(0, w - 14)
                        if w == 18:
                            next_stats(vec, n + 1)
                        if w == 20:
                            next_norm(vec, n + 1)
                        if w in (26, 27):
                            mixed(1, 2 * (w - 26))
                            mixed(1, 2 * (w - 26) + 1)
                        if w == 29:
                            for q in range(4):
                                vec.wait_ge(res_in.sem, res_in.at(n, 64))
                                wait_bank(vec, n, 6, q)
                                vec.tensor_tensor(y_t[:, q, 0:512], P[q][:, :], y_t[:, q, 0:512], ALU.add).then_inc(y_add.sem, 1)
                        if w == 28:
                            vec.memset(lr_t, 1.0).then_inc(lr_ones.sem, 1)
                        if 28 <= w < 32:
                            next_lo(vec, n + 1, 2 * (w - 28))
                            next_lo(vec, n + 1, 2 * (w - 28) + 1)
                        if w == 30:
                            vec.wait_ge(y_add.sem, y_add.at(n, 4))
                            for t in range(TPB):
                                tile_stats(vec, y_t, t, (0,))
                        sample_work(w)
                    for q in range(4):
                        wait_bank(vec, n, 7, q)
                        vec.tensor_tensor(y_t[:, q, 512:1024], P[q][:, :], y_t[:, q, 512:1024], ALU.add).then_inc(y_add.sem, 1)
                        if q > 0:
                            vec.wait_ge(y_add.sem, y_add.at(n, 4 + q))
                            tile_stats(vec, y_t, q - 1, (1,))
                    vec.wait_ge(y_add.sem, y_add.at(n, 8))
                    tile_stats(vec, y_t, TPB - 1, (1,)).then_inc(ystat.sem, 1)
                    mean_square(vec, ystat, n)
                    if kind == 1:
                        sample_residual(1)
                        done(V_X1)
                        sample_stats(l, V_X1)
                    vec.wait_ge(rstd_y.sem, rstd_y.at(n, 1))
                    vec.wait_ge(fin_in.sem, fin_in.at(n, 16))
                    for t in range(TPB):
                        vec.scalar_tensor_tensor(yn[:, t, :], y_t[:, t, :], yrs[:, t:t + 1], fin_w[:, :], ALU.mult, ALU.mult).then_inc(yn_sb.sem, 1)
                    if kind == 1:
                        sample_norm(l, False)

                blocks(vec, l, body)


def rotary_tables():
    row = np.arange(128) % 64
    quarter, second, i = row // 32, (row % 32) // 16, row % 16
    halfdim = DK // 2
    inv = (ROPE_BASE ** (-np.arange(halfdim) / halfdim)).astype(np.float32)
    freq = inv[quarter * 16 + i]
    sign = np.where(second == 1, 1.0, -1.0)
    gamma = 1.0 - 2.0 ** (-5.0 - np.arange(HEADS))

    def tables(pos):
        ang = (pos.astype(np.float32)[None, :] * freq[:, None]).astype(np.float32).astype(np.float64)
        return np.cos(ang), np.sin(ang) * sign[:, None]

    cos, sin = tables(np.arange(SEQ))
    head = np.arange(128) // 64
    out = np.stack([tab.reshape(128, NBLK, BLK).transpose(1, 0, 2) for tab in (cos, sin)], axis=2).astype(np.float32)
    qdec = np.stack([gamma[2 * p + head][:, None] ** (np.arange(TOK) + 1.0)[None, :] for p in range(2)], axis=1).astype(np.float32)
    small = np.zeros((128, 16), np.float32)
    cs, sn = tables(np.array([PAST]))
    small[:, 0], small[:, 1] = cs[:, 0], sn[:, 0]
    small[:, 2], small[:, 3] = cs[:, 0] * DK ** -0.5, sn[:, 0] * DK ** -0.5
    for p in range(2):
        small[:, 4 + p] = gamma[2 * p + head]
        small[:, 6 + p] = gamma[2 * p + head] ** TOK
    return out, qdec, small, gamma


def kernel(x_prompt, x_sample, state_gla, state_ret, norm_w, w_in, gla_w2, gla_b,
           gla_norm_w, ret_norm_w, ret_norm_b, w_out, final_norm_w):
    import concourse.bacc as bacc
    from concourse.bass_utils import run_bass_kernel_spmd

    f = {k: np.asarray(v) for k, v in dict(x_prompt=x_prompt, x_sample=x_sample, state_gla=state_gla, state_ret=state_ret,
         norm_w=norm_w, w_in=w_in, gla_w2=gla_w2, gla_b=gla_b, gla_norm_w=gla_norm_w, ret_norm_w=ret_norm_w,
         ret_norm_b=ret_norm_b, w_out=w_out, final_norm_w=final_norm_w).items()}
    perm = np.arange(64).reshape(2, 2, 16).transpose(1, 0, 2).reshape(64)
    heads_perm = np.concatenate([64 * h + perm for h in range(8)])
    cols = np.cumsum([0, 256, 256, 512, 512, 16, 256, 256, 512, 512])
    w_in, w_out = f["w_in"], f["w_out"]
    slots = np.empty((DEPTH * SLOTS + 3, 128, 1024), np.float32)
    units = [w_in[:, :, cols[5]:cols[7]][:, :, heads_perm], w_in[:, :, cols[7]:cols[8]], w_in[:, :, cols[8]:cols[9]],
             w_in[:, :, 0:512], w_in[:, :, 512:1024], w_in[:, :, 1024:1536],
             np.roll(w_out[:, :, 0:512], -512, axis=1), np.roll(w_out[:, :, 512:1024], -512, axis=1)]
    for l in range(DEPTH):
        gate = w_in[l][:, cols[4]:cols[5]].reshape(2, KT // 2, 128, RANK).transpose(2, 0, 1, 3).reshape(128, 2, GATE // 2)
        slots[l * SLOTS] = 0
        slots[l * SLOTS].reshape(128, 2, 512)[:, :, 0:GATE // 2] = gate
        for u, w in enumerate(units):
            for s in range(4):
                slots[l * SLOTS + 1 + 4 * u + s] = w[l][256 * s:256 * s + 256].reshape(2, 128, 512).transpose(1, 0, 2).reshape(128, 1024)
    slots[DEPTH * SLOTS:] = slots[0:3]
    par = np.empty((DEPTH, 128, 17), np.float32)
    for l in range(DEPTH):
        par[l, :, 0:8] = f["norm_w"][l].reshape(KT, 128).T
        par[l, :, 8] = f["gla_norm_w"][l]
        par[l, :, 9:13] = f["ret_norm_w"][l].reshape(HEADS, DV).T
        par[l, :, 13:17] = f["ret_norm_b"][l].reshape(HEADS, DV).T
    nw_all = np.stack([par[min(m // NBLK, DEPTH - 1), :, 0:8] for m in range(DEPTH * NBLK + 1)])
    w2b = np.concatenate([f["gla_w2"], f["gla_w2"], f["gla_b"][:, None, :]], axis=1)

    def state_in(s, order):
        s = s[:, :, :, order, :].reshape(DEPTH, DECB, 2, 2, 64, DV)
        return np.ascontiguousarray(s.transpose(0, 2, 3, 4, 1, 5).reshape(DEPTH * 2, 128, DECB, DV))

    rope, qdec, small, gamma = rotary_tables()
    s_, t_ = np.arange(TOK)[:, None], np.arange(TOK)[None, :]
    cum = np.zeros((128, 130), np.float32)
    cum[:, 0:128] = ((s_ <= t_).astype(np.float32) - (s_ <= MID)) / TAU
    cum[:, 128:130] = (s_ <= MID) / TAU
    rmask = np.stack([(s_ <= t_) * gamma[h] ** -(s_ + 1.0) * DK ** -0.5 for h in range(HEADS)], axis=1).reshape(128, 512).astype(np.float32)
    kdec = (gamma[None, :] ** (TOK - 1.0 - np.arange(TOK))[:, None] * DK ** -0.5).astype(np.float32)
    comb = np.zeros((16, 64), np.float32)
    for b in range(DECB):
        comb[b, b] = comb[8 + b, b] = 1.0
    ins = dict(
        x_prompt=f["x_prompt"].reshape(SEQ, D), x_sample=f["x_sample"].reshape(DECB, D),
        state_gla=state_in(f["state_gla"], np.arange(64)), state_ret=state_in(f["state_ret"], perm),
        w_slots=slots, par=par, nw_all=nw_all, w2b=w2b, rope=rope, small=small, cum=cum, rmask=rmask, kdec=kdec, qdec=qdec,
        ident=np.eye(128, dtype=np.float32), comb=comb,
        ones=np.full((128, 128), 1.0 / DV, np.float32),
        fin_w=np.broadcast_to(f["final_norm_w"][None, :], (128, D)))
    outs = dict(y_prompt=(SEQ, D), y_sample=(DECB, D), gla_p=(DEPTH, 128, 512), ret_p=(DEPTH, 128, 512),
                gla_s=(DEPTH * 2, 128, DECB, DV), ret_s=(DEPTH * 2, 128, DECB, DV), acts=(SEQ, D), v_s=(DEPTH * 2, DECB, 512))
    nc = bacc.Bacc("TRN2", target_bir_lowering=False, num_devices=1)
    arrays, d = {}, {}
    for name, a in ins.items():
        arrays["in_" + name] = np.ascontiguousarray(a)
        d[name] = nc.dram_tensor("in_" + name, a.shape, mybir.dt.from_np(a.dtype), kind="ExternalInput").ap()
    for name, shape in outs.items():
        kind = "Internal" if name in ("acts", "v_s") else "ExternalOutput"
        d[name] = nc.dram_tensor("out_" + name, shape, mybir.dt.float32, kind=kind).ap()
    build(nc, d)
    r = run_bass_kernel_spmd(nc, [arrays], core_ids=[0]).results[0]
    inv = np.argsort(perm)

    def prompt_state(a, order):
        a = a.reshape(DEPTH, 2, 64, 2, 2, DV)
        a = np.stack([a[:, h % 2, :, h // 2, h % 2, :] for h in range(HEADS)], axis=1)
        return a[:, None, :, order, :]

    def sample_state(a, order):
        a = a.reshape(DEPTH, 2, 2, 64, DECB, DV).transpose(0, 4, 1, 2, 3, 5).reshape(DEPTH, DECB, HEADS, 64, DV)
        return a[:, :, :, order, :]

    same = np.arange(64)
    return (r["out_y_prompt"].reshape(1, SEQ, D), r["out_y_sample"].reshape(DECB, 1, D),
            prompt_state(r["out_gla_p"], same), prompt_state(r["out_ret_p"], inv),
            sample_state(r["out_gla_s"], same), sample_state(r["out_ret_s"], inv))
```
